# Optimizing a Trainium2 kernel written in Bass

```python
import math
import jax, jax.numpy as jnp
from jax import lax
import numpy as np

D_MODEL = 1024
BATCH = 1
SEQ = 256
DEPTH = 2

HEAD_DIM = 64
FOX_HEADS = 4
SB_HEADS = 4
MLA_HEADS = 4
MLA_Q_RANK = 256
MLA_KV_RANK = 128
MLA_NOPE_DIM = 64
MLA_ROPE_DIM = 32
MLA_V_DIM = 128
ROPE_THETA = 10000.0
BLOCK_Q = 128
FOX_W = FOX_HEADS * HEAD_DIM
SB_W = SB_HEADS * HEAD_DIM
MLA_W = MLA_HEADS * MLA_V_DIM
MIX_W = FOX_W + SB_W + MLA_W
IN_SPLITS = (FOX_W, FOX_W, FOX_W, FOX_HEADS, SB_W, SB_W, SB_W, MLA_Q_RANK, MLA_KV_RANK, MLA_ROPE_DIM)
IN_W = sum(IN_SPLITS)

PEER_HEADS = 8
PEER_NKEYS = 128
PEER_EXPERTS = PEER_NKEYS * PEER_NKEYS
PEER_QDIM = 128
PEER_TOPK = 16
TOKEN_CHUNK = 128

PLE_DIM = 256
EPS = 1e-6

kernel_name = "hymba_fox_stickbreak_mla_peer_trunk"

def rms_norm(x, g):
    xf = x.astype(jnp.float32)
    y = xf * lax.rsqrt(jnp.mean(xf * xf, axis=-1, keepdims=True) + EPS)
    return (y * g.astype(jnp.float32)).astype(x.dtype)

def apply_rope(x, pos):
    half = MLA_ROPE_DIM // 2
    inv_freq = ROPE_THETA ** (-jnp.arange(half, dtype=jnp.float32) / half)
    ang = pos.astype(jnp.float32)[..., None] * inv_freq
    ang = ang.reshape(ang.shape[:2] + (1,) * (x.ndim - 3) + (half,))
    cos, sin = jnp.cos(ang), jnp.sin(ang)
    xf = x.astype(jnp.float32)
    x1, x2 = xf[..., :half], xf[..., half:]
    return jnp.concatenate([x1 * cos - x2 * sin, x1 * sin + x2 * cos], axis=-1).astype(x.dtype)

def _split_heads(t, n_heads):
    b, s, _ = t.shape
    return t.reshape(b, s, n_heads, -1).transpose(0, 2, 1, 3)

def _merge_blocks(out):
    nb, b, h, bq, d = out.shape
    return out.transpose(1, 0, 3, 2, 4).reshape(b, nb * bq, h * d)

def causal_softmax_attention(q, k, v, scale, cum_log_f=None):
    s_len = q.shape[2]
    kpos = jnp.arange(s_len)

    def block(i):
        start = i * BLOCK_Q
        qb = lax.dynamic_slice_in_dim(q, start, BLOCK_Q, axis=2)
        qpos = start + jnp.arange(BLOCK_Q)
        logits = jnp.einsum('bhqd,bhkd->bhqk', qb, k, preferred_element_type=jnp.float32) * scale
        if cum_log_f is not None:
            fq = lax.dynamic_slice_in_dim(cum_log_f, start, BLOCK_Q, axis=2)
            logits = logits + fq[..., :, None] - cum_log_f[..., None, :]
        logits = jnp.where(kpos[None, :] <= qpos[:, None], logits, -jnp.inf)
        w = jax.nn.softmax(logits, axis=-1)
        return jnp.einsum('bhqk,bhkd->bhqd', w.astype(v.dtype), v)

    return _merge_blocks(lax.map(block, jnp.arange(s_len // BLOCK_Q)))

def stick_breaking_attention(q, k, v):
    s_len = q.shape[2]
    kpos = jnp.arange(s_len)
    scale = HEAD_DIM ** -0.5

    def block(i):
        start = i * BLOCK_Q
        qb = lax.dynamic_slice_in_dim(q, start, BLOCK_Q, axis=2)
        qpos = start + jnp.arange(BLOCK_Q)
        z = jnp.einsum('bhqd,bhkd->bhqk', qb, k, preferred_element_type=jnp.float32) * scale
        strict = kpos[None, :] < qpos[:, None]
        log_beta = jax.nn.log_sigmoid(z)
        log_one_minus = jnp.where(strict, jax.nn.log_sigmoid(-z), 0.0)
        rest = lax.cumsum(log_one_minus, axis=3, reverse=True) - log_one_minus
        w = jnp.where(strict, jnp.exp(log_beta + rest), 0.0)
        return jnp.einsum('bhqk,bhkd->bhqd', w.astype(v.dtype), v)

    return _merge_blocks(lax.map(block, jnp.arange(s_len // BLOCK_Q)))

def mla_attention(c_q, c_kv, k_rope, pos, q_norm_g, w_uq, kv_norm_g, w_ukv):
    b, s, _ = c_q.shape
    q = (rms_norm(c_q, q_norm_g) @ w_uq).reshape(b, s, MLA_HEADS, MLA_NOPE_DIM + MLA_ROPE_DIM)
    q_nope, q_rot = q[..., :MLA_NOPE_DIM], q[..., MLA_NOPE_DIM:]
    q_rot = apply_rope(q_rot, pos)
    kv = (rms_norm(c_kv, kv_norm_g) @ w_ukv).reshape(b, s, MLA_HEADS, MLA_NOPE_DIM + MLA_V_DIM)
    k_nope, v = kv[..., :MLA_NOPE_DIM], kv[..., MLA_NOPE_DIM:]
    k_rot = jnp.broadcast_to(apply_rope(k_rope, pos)[:, :, None, :], (b, s, MLA_HEADS, MLA_ROPE_DIM))
    q_full = jnp.concatenate([q_nope, q_rot], axis=-1).transpose(0, 2, 1, 3)
    k_full = jnp.concatenate([k_nope, k_rot], axis=-1).transpose(0, 2, 1, 3)
    v = v.transpose(0, 2, 1, 3)
    return causal_softmax_attention(q_full, k_full, v, (MLA_NOPE_DIM + MLA_ROPE_DIM) ** -0.5)

def token_mixer(h, pos, w_in, b_forget, q_norm_g, w_uq, kv_norm_g, w_ukv, out_norm_g, w_o):
    proj = h @ w_in
    offsets = [int(o) for o in np.cumsum(IN_SPLITS)[:-1]]
    fq, fk, fv, f_logit, sq, sk, sv, c_q, c_kv, k_rope = jnp.split(proj, offsets, axis=-1)
    log_f = jax.nn.log_sigmoid(f_logit.astype(jnp.float32) + b_forget.astype(jnp.float32))
    cum_log_f = jnp.cumsum(log_f, axis=1).transpose(0, 2, 1)
    y_fox = causal_softmax_attention(_split_heads(fq, FOX_HEADS), _split_heads(fk, FOX_HEADS),
                                     _split_heads(fv, FOX_HEADS), HEAD_DIM ** -0.5, cum_log_f)
    y_sb = stick_breaking_attention(_split_heads(sq, SB_HEADS), _split_heads(sk, SB_HEADS),
                                    _split_heads(sv, SB_HEADS))
    y_mla = mla_attention(c_q, c_kv, k_rope, pos, q_norm_g, w_uq, kv_norm_g, w_ukv)
    g_fox, g_sb, g_mla = jnp.split(out_norm_g, [FOX_W, FOX_W + SB_W])
    y = jnp.concatenate([rms_norm(y_fox, g_fox), rms_norm(y_sb, g_sb), rms_norm(y_mla, g_mla)], axis=-1)
    return y @ w_o

def peer_ffn(h, w_query, sub_keys, expert_u, expert_v):
    b, s, d = h.shape
    n_chunks = (b * s) // TOKEN_CHUNK
    half = PEER_QDIM // 2

    def chunk(xc):
        c = xc.shape[0]
        q = (xc @ w_query).reshape(c, PEER_HEADS, 2, half)
        scores = jnp.einsum('chpd,hpnd->chpn', q, sub_keys, preferred_element_type=jnp.float32)
        s1, i1 = lax.top_k(scores[:, :, 0], PEER_TOPK)
        s2, i2 = lax.top_k(scores[:, :, 1], PEER_TOPK)
        cand_s = (s1[..., :, None] + s2[..., None, :]).reshape(c, PEER_HEADS, PEER_TOPK * PEER_TOPK)
        cand_id = (i1[..., :, None] * PEER_NKEYS + i2[..., None, :]).reshape(c, PEER_HEADS, PEER_TOPK * PEER_TOPK)
        top_s, top_j = lax.top_k(cand_s, PEER_TOPK)
        ids = jnp.take_along_axis(cand_id, top_j, axis=-1)
        gate = jax.nn.softmax(top_s, axis=-1)
        u = expert_u[ids]
        pre = jnp.einsum('chkd,cd->chk', u, xc, preferred_element_type=jnp.float32)
        act = gate * jax.nn.gelu(pre, approximate=False)
        return jnp.einsum('chk,chkd->cd', act.astype(expert_v.dtype), expert_v[ids])

    out = lax.map(chunk, h.reshape(n_chunks, TOKEN_CHUNK, d))
    return out.reshape(b, s, d)

def per_layer_embedding(h, p_i, w_ple, ple_norm_g, w_ple_gate):
    gate = jax.nn.sigmoid((rms_norm(h, ple_norm_g) @ w_ple_gate).astype(jnp.float32))
    return (gate * (p_i @ w_ple).astype(jnp.float32)).astype(h.dtype)

def setup_inputs(seed: int = 0) -> dict:
    key = jax.random.key(seed)
    ks = jax.random.split(key, 24)
    f32 = jnp.float32

    def normal(k, shape, scale):
        return jax.random.normal(k, shape, f32) * scale

    def gain(k, shape):
        return 1.0 + 0.02 * jax.random.normal(k, shape, f32)

    return {
        "x": normal(ks[0], (BATCH, SEQ, D_MODEL), 1.0),
        "p": normal(ks[1], (DEPTH, BATCH, SEQ, PLE_DIM), 1.0),
        "positions": jnp.broadcast_to(jnp.arange(SEQ, dtype=jnp.int32), (BATCH, SEQ)),
        "norm_mix_g": gain(ks[2], (DEPTH, D_MODEL)),
        "w_in": normal(ks[3], (DEPTH, D_MODEL, IN_W), D_MODEL ** -0.5),
        "b_forget": jax.random.uniform(ks[4], (DEPTH, FOX_HEADS), f32, 1.0, 5.0),
        "mla_q_norm_g": gain(ks[5], (DEPTH, MLA_Q_RANK)),
        "w_uq": normal(ks[6], (DEPTH, MLA_Q_RANK, MLA_HEADS * (MLA_NOPE_DIM + MLA_ROPE_DIM)), MLA_Q_RANK ** -0.5),
        "mla_kv_norm_g": gain(ks[7], (DEPTH, MLA_KV_RANK)),
        "w_ukv": normal(ks[8], (DEPTH, MLA_KV_RANK, MLA_HEADS * (MLA_NOPE_DIM + MLA_V_DIM)), MLA_KV_RANK ** -0.5),
        "mix_out_norm_g": gain(ks[9], (DEPTH, MIX_W)),
        "w_o": normal(ks[10], (DEPTH, MIX_W, D_MODEL), MIX_W ** -0.5),
        "norm_ffn_g": gain(ks[11], (DEPTH, D_MODEL)),
        "peer_w_query": normal(ks[12], (DEPTH, D_MODEL, PEER_HEADS * PEER_QDIM), D_MODEL ** -0.5),
        "peer_sub_keys": normal(ks[13], (DEPTH, PEER_HEADS, 2, PEER_NKEYS, PEER_QDIM // 2), (PEER_QDIM // 2) ** -0.5),
        "peer_u": normal(ks[14], (DEPTH, PEER_EXPERTS, D_MODEL), D_MODEL ** -0.5),
        "peer_v": normal(ks[15], (DEPTH, PEER_EXPERTS, D_MODEL), PEER_HEADS ** -0.5),
        "w_ple": normal(ks[16], (DEPTH, PLE_DIM, D_MODEL), PLE_DIM ** -0.5),
        "ple_norm_g": gain(ks[17], (DEPTH, D_MODEL)),
        "w_ple_gate": normal(ks[18], (DEPTH, D_MODEL, D_MODEL), D_MODEL ** -0.5),
        "final_norm_g": gain(ks[19], (D_MODEL,)),
    }

def reference(x, p, positions, norm_mix_g, w_in, b_forget, mla_q_norm_g, w_uq, mla_kv_norm_g, w_ukv,
              mix_out_norm_g, w_o, norm_ffn_g, peer_w_query, peer_sub_keys, peer_u, peer_v,
              w_ple, ple_norm_g, w_ple_gate, final_norm_g):
    h = x
    for i in range(DEPTH):
        h = h + token_mixer(rms_norm(h, norm_mix_g[i]), positions, w_in[i], b_forget[i],
                            mla_q_norm_g[i], w_uq[i], mla_kv_norm_g[i], w_ukv[i],
                            mix_out_norm_g[i], w_o[i])
        h = h + peer_ffn(rms_norm(h, norm_ffn_g[i]), peer_w_query[i], peer_sub_keys[i], peer_u[i], peer_v[i])
        h = h + per_layer_embedding(h, p[i], w_ple[i], ple_norm_g[i], w_ple_gate[i])
    return rms_norm(h, final_norm_g)


_drawn_inputs = setup_inputs


def setup_inputs(seed=0):
    import zlib

    import numpy as np

    out = dict(_drawn_inputs(seed))
    spreads = {}
    factors = {'mla_q_norm_g': 2.987, 'ple_norm_g': 24.427, 'final_norm_g': 8.086}
    for name, (base, spread) in spreads.items():
        noise = np.random.default_rng([zlib.crc32(name.encode()), seed]).standard_normal(out[name].shape)
        drawn = base * np.exp(spread * noise) if base else spread * noise
        out[name] = __import__('jax').numpy.asarray(drawn.astype(out[name].dtype))
    for name, factor in factors.items():
        out[name] = (out[name] * factor).astype(out[name].dtype)
    return out
```

```python
from contextlib import ExitStack

import numpy as np
import concourse.bass as bass
from concourse import mybir

ALU = mybir.AluOpType
ACT = mybir.ActivationFunctionType
AX_X = mybir.AxisListType.X
F32 = mybir.dt.float32
I32 = mybir.dt.int32
U32 = mybir.dt.uint32

P = 128
D = 1024
KT = D // P
SEQ, TILES, DEPTH = 256, 2, 2
STEPS = DEPTH * TILES
HEADS, HD = 4, 64
NOPE, ROPE, VD = 64, 32, 128
QK = NOPE + ROPE
QR, KVR = 256, 128
FOX_SCALE, MLA_SCALE = HD ** -0.5, QK ** -0.5
IN_W = 3 * 256 + 4 + 3 * 256 + QR + KVR + ROPE
EPS = 1e-6
PH, NKEY, TOPK = 8, 128, 16
EXPERTS = NKEY * NKEY
PAIRS = PH * TOPK
RING, GROUP = 8, 4
GROUPS = PAIRS // GROUP
WRING, WSLOT = 4, 2048
NEG = -1e30
HALF = ROPE // 2
C_ID, C_LE, C_GT, C_ONE, C_CAUSAL, C_STRICT, C_SEL, C_FREQ, C_IOTA = 0, 128, 256, 384, 512, 640, 768, 1280, 1296
C_W = 1312
G_MIX, G_Q, G_KV, G_OUT, G_PLE, G_W = 0, 8, 10, 11, 19, 27

MIX_LOADS = [("in", k) for k in range(KT)] + [("latent", 0)] + [("out", k) for k in range(KT // 2)] + \
            [("query", k) for k in range(KT // 2)] + [("keys", 0)]
EMBED_LOADS = [("ple", 0)] + [("gate", k) for k in range(KT // 2)]


def layer_tile(s):
    return s // TILES, s % TILES


def weight_order():
    order = [(kind, k, 0) for kind, k in MIX_LOADS]
    for w in range(STEPS):
        if w >= 1:
            order += [(kind, k, w - 1) for kind, k in EMBED_LOADS]
        if w + 1 < STEPS:
            order += [(kind, k, w + 1) for kind, k in MIX_LOADS]
    return order + [(kind, k, STEPS - 1) for kind, k in EMBED_LOADS]


class Shares:

    def __init__(self, stream, step, turns):
        self.stream, self.step, self.turns, self.n = stream, step, turns, 0

    def __call__(self):
        a = self.n * GROUPS // self.turns
        self.n += 1
        b = self.n * GROUPS // self.turns
        assert self.n <= self.turns
        self.stream(self.step, a, b)

    def rest(self):
        while self.n < self.turns:
            self()


MIX_TURNS, EMBED_TURNS = 25, 3


def window_turns(w):
    n = (EMBED_TURNS if w >= 1 else 0) + (MIX_TURNS if w + 1 < STEPS else 0)
    return n + 1


def share_out(stream, step, a, b):
    if a % 2 and a < b:
        stream.group(step, a // 2, 1)
        a += 1
    if b - a >= 4:
        stream.loop(step, a // 2, b // 2)
        a = b // 2 * 2
    while a < b:
        stream.group(step, a // 2, a % 2)
        a += 1


class Stream:

    def __init__(self, eng, body):
        self.eng, self.body = eng, body

    def group(self, step, i, half):
        self.body(step, i, half)

    def loop(self, step, lo, hi):
        with self.eng.Fori(lo, hi) as i:
            for half in range(2):
                self.body(step, i, half)

    def __call__(self, step, a, b):
        share_out(self, step, a, b)


def walk(stream, mix, embed, finish, begin):
    mix(0, lambda: None)
    for w in range(STEPS):
        begin(w)
        turn = Shares(stream, w, window_turns(w))
        if w >= 1:
            embed(w - 1, turn)
        if w + 1 < STEPS:
            mix(w + 1, turn)
        else:
            finish(0)
        turn.rest()
    begin(STEPS)
    embed(STEPS - 1, lambda: None)
    finish(1)


def trunk(nc, x, p_t, pos, gains, forget_b, ffn_g, final_g, w_in, w_latent, w_out, w_query, keys,
          rows, w_ple, w_gate, consts, out):
    with ExitStack() as ctx:
        def sb(name, shape, dt=F32):
            return ctx.enter_context(nc.sbuf_tensor(name, shape, dt))

        def sem(name):
            return ctx.enter_context(nc.semaphore(name))

        ring = sb("ring", [P, RING, 2 * D])
        wring = sb("wring", [P, WRING, WSLOT])
        h = sb("h", [P, TILES, D])
        rows_n = sb("rows_n", [P, D])
        hT = sb("hT", [P, KT, P])
        y = sb("y", [P, D])
        xc = sb("xc", [P, 2, D])
        wa = sb("wa", [P, 2048])
        wb = sb("wb", [P, 2048])
        cst = sb("cst", [P, C_W])
        gn = sb("gn", [P, DEPTH, G_W])
        fb = sb("fb", [P, DEPTH, HEADS])
        gffn = sb("gffn", [P, DEPTH, D])
        gfin = sb("gfin", [P, D])
        pT = sb("pT", [P, DEPTH * 2, SEQ])
        posi = sb("posi", [P, TILES], I32)
        posf = sb("posf", [P, TILES])
        ang = sb("ang", [P, TILES, HALF])
        turns_n = sb("turns_n", [P, TILES, HALF])
        sin = sb("sin", [P, TILES, HALF])
        cos = sb("cos", [P, TILES, HALF])
        qTf = sb("qTf", [P, HEADS, P])
        kTf = sb("kTf", [P, 2, SEQ])
        qTs = sb("qTs", [P, HEADS, P])
        kTs = sb("kTs", [P, 2, SEQ])
        vf = sb("vf", [P, TILES, 256])
        vs = sb("vs", [P, TILES, 256])
        qTm = sb("qTm", [P, HEADS, P])
        kTm = sb("kTm", [P, HEADS, SEQ])
        vm = sb("vm", [P, TILES, HEADS, VD])
        zf = sb("zf", [P, 3, HEADS])
        logf = sb("logf", [P, TILES, HEADS])
        F8 = sb("F8", [P, HEADS])
        FT = sb("FT", [P, SEQ])
        lat = sb("lat", [P, QR + KVR])
        latT = sb("latT", [P, 3, P])
        qf = sb("qf", [P, HEADS, QK])
        kf = sb("kf", [P, HEADS, QK])
        rot = sb("rot", [P, HEADS + 1, ROPE])
        rot_p = sb("rot_p", [P, 4, HEADS + 1, HALF])
        rotated = sb("rotated", [P, HEADS + 1, ROPE])
        peak = sb("peak", [P, 2, HEADS])
        den = sb("den", [P, 2, HEADS])
        ssq = sb("ssq", [P, 3])
        inv = sb("inv", [P, 4, 3])
        top_v = sb("top_v", [P, 2 * PH, TOPK])
        top_i = sb("top_i", [P, 2 * PH, TOPK], U32)
        top_f = sb("top_f", [P, 2 * PH, TOPK])
        best_v = sb("best_v", [P, PH, TOPK])
        best_i = sb("best_i", [P, PH, TOPK], U32)
        part_i = sb("part_i", [P, 2, PH, TOPK], U32)
        part_f = sb("part_f", [P, 2, PH, TOPK])
        part_id = sb("part_id", [P, 2, PH, TOPK])
        gsum = sb("gsum", [P, 2, PH])
        gate = sb("gate", [P, 2, PAIRS])
        ids = sb("ids", [P, 2, PAIRS], I32)
        pre = sb("pre", [P, RING])
        gel = sb("gel", [P, RING])
        act_w = sb("act_w", [P, RING])
        diag = sb("diag", [P, RING, P])

        acc = ctx.enter_context(nc.psum_tensor("acc", [P, 2, 512], F32))
        bank = [ctx.enter_context(nc.psum_tensor(f"bank{i}", [P, 512], F32)) for i in range(6)]

        ident = cst[:, C_ID:C_ID + P]
        tri_le = cst[:, C_LE:C_LE + P]
        tri_gt = cst[:, C_GT:C_GT + P]
        ones = cst[:, C_ONE:C_ONE + P]
        causal = cst[:, C_CAUSAL:C_CAUSAL + P]
        strict = cst[:, C_STRICT:C_STRICT + P]
        iota = cst[:, C_IOTA:C_IOTA + TOPK]
        fox_s = wa[:, 0:1024].rearrange("p (h k) -> p h k", h=HEADS)
        probsT = wa[:, 1024:2048].rearrange("p (t c) -> p t c", t=2)
        soft = wa[:, 0:1024].rearrange("p (t c) -> p t c", t=2)
        logb = wb[:, 0:1024].rearrange("p (t c) -> p t c", t=2)
        lom = wb[:, 1024:2048].rearrange("p (t c) -> p t c", t=2)
        mla_s = wb[:, 0:1024].rearrange("p (h k) -> p h k", h=HEADS)
        gate_s = wb[:, 0:1024]
        queryT = y[:, :].rearrange("p (h c) -> p h c", h=PH)

        def score(hp):
            hd, half = divmod(hp, 2)
            return bank[4 * half + hd // 4][:, hd % 4 * P:hd % 4 * P + P]

        consts_in = sem("consts_in")
        late_in = sem("late_in")
        weight_in = [sem(f"weight_in{i}") for i in range(WRING)]
        weight_used = sem("weight_used")
        row_in = [sem(f"row_in{i}") for i in range(RING)]
        dotted = sem("dotted")
        gelued = sem("gelued")
        weighted = sem("weighted")
        diag_ready = sem("diag_ready")
        row_used = sem("row_used")
        acc_init = sem("acc_init")
        acc_read = sem("acc_read")
        ids_ready = sem("ids_ready")
        gate_ready = sem("gate_ready")
        dve_done = sem("dve_done")
        act_done = sem("act_done")
        zeroed = sem("zeroed")
        angles_ready = sem("angles_ready")
        trig_ready = sem("trig_ready")
        normed = sem("normed")
        turned = sem("turned")
        hT_ready = sem("hT_ready")
        heads_ready = sem("heads_ready")
        forget_in = sem("forget_in")
        forget_ln = sem("forget_ln")
        latents_left = sem("latents_left")
        logf_ready = sem("logf_ready")
        cum_ready = sem("cum_ready")
        latT_ready = sem("latT_ready")
        latent_copied = sem("latent_copied")
        rotated_ready = sem("rotated_ready")
        full_turned = sem("full_turned")
        full_ready = sem("full_ready")
        scored = sem("scored")
        peak_ready = sem("peak_ready")
        probs_ready = sem("probs_ready")
        probs_turned = sem("probs_turned")
        probsT_ready = sem("probsT_ready")
        stick_scored = sem("stick_scored")
        soft_ready = sem("soft_ready")
        lom_ready = sem("lom_ready")
        rest_ready = sem("rest_ready")
        stick_sum = sem("stick_sum")
        stick_exp = sem("stick_exp")
        stick_ready = sem("stick_ready")
        attended = sem("attended")
        query_ready = sem("query_ready")
        gate_in = sem("gate_in")
        gate_exp = sem("gate_exp")
        sig_ready = sem("sig_ready")
        result_ready = sem("result_ready")
        stored = sem("stored")

        order = weight_order()
        block = ctx.enter_context(nc.Block())

        def wait_products(eng, kind, s):
            eng.wait_ge(weight_used, 1 + max(n for n, (a, _, b) in enumerate(order) if (a, b) == (kind, s)))

        def waiter(eng):
            seen = {}

            def next_of(s, n=1):
                seen[s.name] = seen.get(s.name, 0) + n
                eng.wait_ge(s, seen[s.name])
            return next_of

        @block.sync
        def _(sp):
            for dst, src in ((h[:, 0, :], x[0:P, :]), (cst[:], consts), (gn[:], gains),
                             (fb[:], forget_b.partition_broadcast(P)), (posi[:], pos)):
                sp.dma_start(dst, src).then_inc(consts_in, 16)
            source = {
                "in": lambda l, k: w_in[l, k * P:(k + 1) * P, :],
                "latent": lambda l, k: w_latent[l],
                "out": lambda l, k: w_out[l, 2 * k * P:2 * (k + 1) * P, :].rearrange("(a p) n -> p a n", p=P),
                "query": lambda l, k: w_query[l, 2 * k * P:2 * (k + 1) * P, :].rearrange("(a p) n -> p a n", p=P),
                "gate": lambda l, k: w_gate[l, 2 * k * P:2 * (k + 1) * P, :].rearrange("(a p) n -> p a n", p=P),
                "ple": lambda l, k: w_ple[l].rearrange("(a p) n -> p a n", p=P),
                "keys": lambda l, k: keys[l],
            }
            for n, (kind, k, s) in enumerate(order):
                if n >= WRING:
                    sp.wait_ge(weight_used, n - WRING + 1)
                src = source[kind](layer_tile(s)[0], k)
                if len(src.shape) == 3:
                    dst = wring[:, n % WRING, :].rearrange("p (a n) -> p a n", a=2)
                else:
                    dst = wring[:, n % WRING, 0:src.shape[1]]
                sp.dma_start(dst, src).then_inc(weight_in[n % WRING], 16)
                if n == WRING - 1:
                    for dst, src in ((h[:, 1, :], x[P:2 * P, :]), (gffn[:], ffn_g.partition_broadcast(P)),
                                     (gfin[:], final_g.partition_broadcast(P)),
                                     (pT[:], p_t.rearrange("(a p) s -> p a s", p=P))):
                        sp.dma_start(dst, src).then_inc(late_in, 16)
            for t in range(TILES):
                sp.wait_ge(result_ready, t + 1)
                sp.dma_start(out[t * P:(t + 1) * P, :], (y, rows_n)[t][:, :]).then_inc(stored, 16)
            sp.wait_ge(stored, 16 * TILES)

        @block.gpsimd
        def _(pool):
            for n in range(STEPS * PAIRS):
                w, k = divmod(n, PAIRS)
                if k == 0:
                    pool.wait_ge(ids_ready, w + 1)
                if n >= RING:
                    pool.wait_ge(row_used, n - RING + 1)
                pool.indirect_dma_start(
                    out=ring[:, n % RING, :], out_offset=None, in_=rows,
                    in_offset=bass.IndirectOffsetOnAxis(ap=ids[:, w % 2, k:k + 1], axis=0),
                ).then_inc(row_in[n % RING], 16)

        @block.tensor
        def _(pe):
            next_of = waiter(pe)
            used = [0]

            def weights():
                n = used[0]
                pe.wait_ge(weight_in[n % WRING], 16 * (n // WRING + 1))
                return wring[:, n % WRING, :]

            def release(last):
                used[0] += 1
                last.then_inc(weight_used, 1)

            def experts(step, i, half):
                for j in range(half * GROUP, half * GROUP + GROUP):
                    pe.wait_ge(diag_ready, step * PAIRS + i * RING + j + 1)
                    for c in range(2):
                        last = pe.matmul(acc[:, c, :], diag[:, j, :], ring[:, j, D + c * 512:D + c * 512 + 512],
                                         start=False, stop=True, skip_group_check=True)
                    last.then_inc(row_used, 1)

            def begin(w):
                if w == STEPS:
                    return
                if w >= 1:
                    pe.wait_ge(acc_read, 2 * w)
                for c in range(2):
                    pe.matmul(acc[:, c, :], ident, h[:, w % 2, c * 512:c * 512 + 512],
                              start=True, stop=True, skip_group_check=True)

            def turn_rows(src):
                for k in range(KT):
                    last = pe.transpose(bank[k // 4][:, k % 4 * P:k % 4 * P + P], src[:, k * P:(k + 1) * P], ident)
                last.then_inc(turned, 1)

            def rows_times(wide, banks, slabs, turn):
                for k in range(slabs // 2):
                    w = weights()
                    for a in range(2):
                        for c in range(2):
                            last = pe.matmul(banks[c][:, :], wide(2 * k + a), w[:, a * D + c * 512:a * D + c * 512 + 512],
                                             start=(k == 0 and a == 0), stop=(2 * k + a == slabs - 1),
                                             skip_group_check=True)
                    release(last)
                    if slabs == KT and k == 1:
                        turn()
                return last

            def head_scores(s, qT, kT, width, fox):
                l, t = layer_tile(s)
                for kt in range(t + 1):
                    for hd in range(HEADS):
                        o = bank[kt][:, hd * P:(hd + 1) * P]
                        keys_at = slice(kt * P, (kt + 1) * P)
                        if fox:
                            pe.matmul(o, qT[:, hd, :], kT[:, hd // 2, keys_at], start=True, stop=False)
                            last = pe.matmul(o, cst[:, C_SEL + hd * P:C_SEL + (hd + 1) * P], FT[:, keys_at],
                                             start=False, stop=True)
                        else:
                            last = pe.matmul(o, qT[0:width, hd, :], kT[0:width, hd, keys_at], start=True, stop=True)
                last.then_inc(scored, 1)

            def turn_probs(s, src):
                l, t = layer_tile(s)
                next_of(probs_ready, HEADS)
                for kt in range(t + 1):
                    for hd in range(HEADS):
                        last = pe.transpose(bank[2 + kt][:, hd * P:(hd + 1) * P], src[:, hd, kt * P:(kt + 1) * P], ident)
                last.then_inc(probs_turned, 1)

            def weigh(s, dst, src, v, width):
                l, t = layer_tile(s)
                for hd in range(HEADS):
                    for kt in range(t + 1):
                        last = pe.matmul(dst[:, hd * width:(hd + 1) * width], src[:, kt, hd * P:(hd + 1) * P],
                                         v(kt, hd), start=(kt == 0), stop=(kt == t))
                last.then_inc(attended, 1)

            def mix(s, turn):
                l, t = layer_tile(s)
                if s == 0:
                    pe.wait_ge(consts_in, 80)
                next_of(normed)
                turn_rows(rows_n)
                turn()
                next_of(hT_ready, 2)
                for k in range(KT):
                    w = weights()
                    a, z = k == 0, k == KT - 1
                    for i, (b, col) in enumerate([(b, c) for b in (2, 3) for c in range(4)]):
                        c0 = (0 if b == 2 else 772) + col * P
                        pe.matmul(bank[b][:, col * P:(col + 1) * P], w[:, c0:c0 + P], hT[:, k, :],
                                  start=(a and col == 0), stop=z, skip_group_check=True)
                    pe.matmul(bank[4][:, 0:260], hT[:, k, :], w[:, 512:772], start=a, stop=z, skip_group_check=True)
                    pe.matmul(bank[4][:, 260:420], hT[:, k, :], w[:, 1796:1956], start=False, stop=z, skip_group_check=True)
                    last = pe.matmul(bank[5][:, :], hT[:, k, :], w[:, 1284:1796], start=a, stop=z, skip_group_check=True)
                    release(last)
                    if k % 2 and k < KT - 1:
                        turn()
                turn()
                next_of(logf_ready)
                pe.matmul(bank[0][:, 0:HEADS], tri_le, logf[:, t, :], start=True, stop=(t == 0))
                if t:
                    pe.matmul(bank[0][:, 0:HEADS], ones, logf[:, 0, :], start=False, stop=True)
                pe.matmul(bank[0][0:HEADS, P:2 * P], logf[:, t, :], tri_le, start=True, stop=(t == 0))
                if t:
                    pe.matmul(bank[0][0:HEADS, P:2 * P], logf[:, 0, :], ones, start=False, stop=True)
                next_of(normed)
                for k in range(3):
                    last = pe.transpose(bank[1][:, k * P:(k + 1) * P], lat[:, k * P:(k + 1) * P], ident)
                last.then_inc(cum_ready, 1)
                turn()
                next_of(latT_ready)
                next_of(heads_ready, 8)
                w = weights()
                for k in range(2):
                    pe.matmul(bank[2][:, 0:384], latT[:, k, :], w[:, k * 384:(k + 1) * 384], start=(k == 0), stop=(k == 1))
                for c in range(2):
                    last = pe.matmul(bank[3 + c][:, 0:384], latT[:, 2, :], w[:, 768 + c * 384:768 + (c + 1) * 384],
                                     start=True, stop=True)
                release(last)
                turn()
                head_scores(s, qTf, kTf, HD, True)
                next_of(rotated_ready)
                next_of(latent_copied, 4)
                for b, src in ((4, qf), (5, kf)):
                    for hd in range(HEADS):
                        last = pe.transpose(bank[b][0:QK, hd * P:(hd + 1) * P], src[:, hd, :], ident)
                last.then_inc(full_turned, 1)
                turn()
                turn_probs(s, fox_s)
                for kt in range(t + 1):
                    for pair in range(HEADS // 2):
                        last = pe.matmul(bank[kt][:, pair * 2 * P:(pair + 1) * 2 * P], kTs[:, pair, kt * P:(kt + 1) * P],
                                         qTs[:, 2 * pair:2 * pair + 2, :], start=True, stop=True)
                last.then_inc(stick_scored, 1)
                turn()
                next_of(probsT_ready, t + 1)
                next_of(full_ready, 2)
                weigh(s, bank[4], probsT, lambda kt, hd: vf[:, kt, hd * HD:(hd + 1) * HD], HD)
                next_of(lom_ready)
                for kt in range(t + 1):
                    last = pe.matmul(bank[2 + kt][:, :], tri_gt, lom[:, kt, :], start=True, stop=(kt == t))
                    for later in range(kt + 1, t + 1):
                        last = pe.matmul(bank[2 + kt][:, :], ones, lom[:, later, :], start=False, stop=(later == t))
                last.then_inc(rest_ready, 1)
                turn()
                head_scores(s, qTm, kTm, QK, False)
                next_of(stick_ready)
                weigh(s, bank[4][:, 256:512], soft, lambda kt, hd: vs[:, kt, hd * HD:(hd + 1) * HD], HD)
                turn()
                turn_probs(s, mla_s)
                turn()
                next_of(probsT_ready, t + 1)
                weigh(s, bank[5], probsT, lambda kt, hd: vm[:, kt, hd, :], VD)
                turn()
                next_of(normed)
                turn_rows(rows_n)
                turn()
                next_of(hT_ready, 2)
                rows_times(lambda k: hT[:, k, :], (bank[2], bank[3]), KT, turn)
                turn()
                next_of(normed)
                turn_rows(xc[:, s % 2, :])
                turn()
                next_of(hT_ready, 2)
                for k in range(KT // 2):
                    w = weights()
                    for a in range(2):
                        for hd in range(PH):
                            last = pe.matmul(bank[2 + hd // 4][:, hd % 4 * P:hd % 4 * P + P],
                                             w[:, a * D + hd * P:a * D + (hd + 1) * P], hT[:, 2 * k + a, :],
                                             start=(k == 0 and a == 0 and hd % 4 == 0),
                                             stop=(k == KT // 2 - 1 and a == 1), skip_group_check=True)
                    release(last)
                    if k == 1:
                        turn()
                turn()
                next_of(query_ready, 2)
                w = weights()
                for hp in range(2 * PH):
                    b = hp % 2 * 64
                    last = pe.matmul(score(hp), queryT[b:b + 64, hp // 2, :], w[b:b + 64, hp // 2 * P:(hp // 2 + 1) * P],
                                     start=True, stop=True)
                release(last)
                for _ in range(6):
                    turn()

            def embed(s, turn):
                l, t = layer_tile(s)
                next_of(normed)
                turn_rows(rows_n)
                turn()
                if s == 0:
                    pe.wait_ge(late_in, 64)
                rows_times(lambda k: pT[:, 2 * l + k, t * P:(t + 1) * P], (bank[4], bank[5]), 2, turn)
                next_of(hT_ready, 2)
                rows_times(lambda k: hT[:, k, :], (bank[2], bank[3]), KT, turn)
                turn()

            walk(Stream(pe, experts), mix, embed, lambda t: None, begin)

        @block.scalar
        def _(act):
            next_of = waiter(act)

            def experts(step, i, half):
                j0 = half * GROUP
                cols = bass.ds(i * RING + j0, GROUP)
                act.wait_ge(dotted, step * PAIRS + i * RING + j0 + GROUP)
                act.activation(gel[:, j0:j0 + GROUP], pre[:, j0:j0 + GROUP], ACT.Gelu).then_inc(gelued, 1)
                act.wait_ge(gelued, step * GROUPS + 2 * i + half + 1)
                for j in range(j0, j0 + GROUP):
                    last = act.activation(act_w[:, j:j + 1], gate[:, step % 2, bass.ds(i * RING + j, 1)], ACT.Copy,
                                          scale=gel[:, j:j + 1])
                last.then_inc(weighted, 1)
                act.wait_ge(weighted, step * GROUPS + 2 * i + half + 1)
                for j in range(j0, j0 + GROUP):
                    act.activation(diag[:, j, :], ident, ACT.Copy, scale=act_w[:, j:j + 1]).then_inc(diag_ready, 1)

            def begin(w):
                if w < STEPS:
                    act.wait_ge(gate_ready, w + 1)

            def exps(s, src, slot, scale):
                l, t = layer_tile(s)
                next_of(peak_ready)
                for hd in range(HEADS):
                    act.activation(src[:, hd, 0:(t + 1) * P], src[:, hd, 0:(t + 1) * P], ACT.Exp,
                                   bias=peak[:, slot, hd:hd + 1], scale=scale,
                                   accum_out=den[:, slot, hd:hd + 1]).then_inc(probs_ready, 1)

            def copy_probsT(s):
                l, t = layer_tile(s)
                next_of(probs_turned)
                for kt in range(t + 1):
                    act.activation(probsT[:, kt, :], bank[2 + kt][:, :], ACT.Copy).then_inc(probsT_ready, 1)

            def mix(s, turn):
                l, t = layer_tile(s)
                here = slice(t * P, (t + 1) * P)
                if s == 0:
                    act.wait_ge(angles_ready, 2)
                    act.activation(sin[:], ang[:], ACT.Sin).then_inc(trig_ready, 1)
                    act.activation(cos[:], turns_n[:], ACT.Sin).then_inc(trig_ready, 1)
                turn()
                for _ in range(4):
                    turn()
                if s == 0:
                    act.wait_ge(zeroed, 3)
                wait_products(act, "in", s)
                for b, qT, kT in ((bank[2], qTf, kTf), (bank[3], qTs, kTs)):
                    q2 = b[:, 0:256].rearrange("p (g c) -> p g c", g=2)
                    pairs = qT[:].rearrange("p (g two) c -> p g two c", two=2)
                    for half in range(2):
                        r = slice(half * HD, (half + 1) * HD)
                        act.activation(pairs[r, :, half, :], q2[r, :, :], ACT.Copy).then_inc(heads_ready, 1)
                    act.activation(kT[:, :, here], b[:, 256:512].rearrange("p (g c) -> p g c", g=2),
                                   ACT.Copy).then_inc(heads_ready, 1)
                next_of(forget_in)
                act.activation(zf[:, 2, :], zf[:, 1, :], ACT.Exp, scale=-1.0).then_inc(act_done, 1)
                next_of(act_done)
                act.activation(zf[:, 2, :], zf[:, 2, :], ACT.Ln, bias=1.0).then_inc(forget_ln, 1)
                next_of(latents_left)
                for dst, src in ((vf[:, t, :], bank[4][:, 0:256]), (vs[:, t, :], bank[5][:, 0:256])):
                    act.activation(dst, src, ACT.Copy).then_inc(heads_ready, 1)
                turn()
                turn()
                wait_products(act, "latent", s)
                for c in range(2):
                    kv = bank[3 + c][:, 0:384].rearrange("p (h c) -> p h c", h=2)
                    act.activation(kf[:, 2 * c:2 * c + 2, 0:NOPE], kv[:, :, 0:NOPE], ACT.Copy).then_inc(latent_copied, 1)
                    act.activation(vm[:, t, 2 * c:2 * c + 2, :], kv[:, :, NOPE:NOPE + VD], ACT.Copy).then_inc(latent_copied, 1)
                turn()
                exps(s, fox_s, 0, FOX_SCALE)
                next_of(full_turned)
                act.activation(qTm[0:QK, :, :], bank[4][0:QK, :].rearrange("p (h c) -> p h c", h=HEADS),
                               ACT.Copy).then_inc(full_ready, 1)
                act.activation(kTm[0:QK, :, here], bank[5][0:QK, :].rearrange("p (h c) -> p h c", h=HEADS),
                               ACT.Copy).then_inc(full_ready, 1)
                turn()
                copy_probsT(s)
                next_of(stick_scored)
                for kt in range(t + 1):
                    act.activation(soft[:, kt, :], bank[kt][:, :], ACT.Abs, scale=FOX_SCALE).then_inc(act_done, 1)
                next_of(act_done, t + 1)
                for kt in range(t + 1):
                    act.activation(soft[:, kt, :], soft[:, kt, :], ACT.Exp, scale=-1.0).then_inc(act_done, 1)
                next_of(act_done, t + 1)
                for kt in range(t + 1):
                    act.activation(soft[:, kt, :], soft[:, kt, :], ACT.Ln, bias=1.0).then_inc(soft_ready, 1)
                turn()
                next_of(stick_sum)
                for kt in range(t + 1):
                    act.activation(soft[:, kt, :], logb[:, kt, :], ACT.Exp).then_inc(stick_exp, 1)
                turn()
                exps(s, mla_s, 1, MLA_SCALE)
                turn()
                copy_probsT(s)
                turn()
                turn()
                turn()
                turn()
                turn()
                turn()
                turn()
                wait_products(act, "query", s)
                for c in range(2):
                    act.activation(queryT[:, 4 * c:4 * c + 4, :], bank[2 + c][:, :].rearrange("p (h c) -> p h c", h=4),
                                   ACT.Copy).then_inc(query_ready, 1)
                turn()
                turn()
                for _ in range(5):
                    turn()
                next_of(gate_in)
                act.activation(best_v[:], best_v[:], ACT.Exp).then_inc(gate_exp, 1)

            def embed(s, turn):
                turn()
                turn()
                turn()
                wait_products(act, "gate", s)
                for c in range(2):
                    act.activation(gate_s[:, c * 512:(c + 1) * 512], bank[2 + c][:, :], ACT.Sigmoid).then_inc(sig_ready, 1)

            walk(Stream(act, experts), mix, embed, lambda t: None, begin)

        @block.vector
        def _(dve):
            next_of = waiter(dve)

            def link(ins):
                ins.then_inc(dve_done, 1)
                next_of(dve_done)

            def experts(step, i, half):
                for j in range(half * GROUP, half * GROUP + GROUP):
                    dve.wait_ge(row_in[j], (step * (PAIRS // RING) + i + 1) * 16)
                    u = ring[:, j, 0:D]
                    dve.tensor_tensor_reduce(out=u, in0=u, in1=xc[:, step % 2, :], scale=1.0, scalar=0.0,
                                             op0=ALU.mult, op1=ALU.add, accum_out=pre[:, j:j + 1]).then_inc(dotted, 1)

            def rsqrt(sizes):
                n = len(sizes)
                v, g, a, b = (inv[:, i, 0:n] for i in range(4))
                for i, size in enumerate(sizes):
                    link(dve.tensor_scalar(inv[:, 0, i:i + 1], ssq[:, i:i + 1], 1.0 / size, EPS, ALU.mult, ALU.add))
                link(dve.tensor_scalar(g.bitcast(U32), v.bitcast(U32), 1, None, ALU.logical_shift_right))
                link(dve.tensor_scalar(g.bitcast(I32), g.bitcast(I32), -1.0, float(0x5f3759df), ALU.mult, ALU.add))
                for _ in range(4):
                    link(dve.tensor_tensor(a, g, v, ALU.mult))
                    link(dve.scalar_tensor_tensor(out=b, in0=a, scalar=-0.5, in1=g, op0=ALU.mult, op1=ALU.mult))
                    link(dve.scalar_tensor_tensor(out=g, in0=b, scalar=1.5, in1=g, op0=ALU.add, op1=ALU.mult))

            def squares(src, i, junk):
                link(dve.tensor_tensor_reduce(out=junk, in0=src, in1=src, scale=1.0, scalar=0.0,
                                              op0=ALU.mult, op1=ALU.add, accum_out=ssq[:, i:i + 1]))

            def norm_rows(src):
                squares(src, 0, rows_n[:, :])
                rsqrt([D])
                dve.tensor_scalar(rows_n[:, :], src, inv[:, 1, 0:1], None, ALU.mult).then_inc(normed, 1)

            def copy_hT(gain):
                next_of(turned)
                for c in range(2):
                    src = bank[c][:, :].rearrange("p (k c) -> p k c", k=4)
                    if gain is None:
                        ins = dve.tensor_copy(hT[:, 4 * c:4 * c + 4, :], src)
                    else:
                        g = gain[:, 4 * c:4 * c + 4].unsqueeze(2).broadcast_to([P, 4, P])
                        ins = dve.tensor_tensor(hT[:, 4 * c:4 * c + 4, :], src, g, ALU.mult)
                    ins.then_inc(hT_ready, 1)

            def peaks(s, dst, slot, scale, fox):
                l, t = layer_tile(s)
                next_of(scored)
                for kt in range(t + 1):
                    src = bank[kt][:, :].rearrange("p (h k) -> p h k", h=HEADS)
                    o = dst[:, :, kt * P:(kt + 1) * P]
                    mask = causal.unsqueeze(1).broadcast_to([P, HEADS, P])
                    if fox:
                        link(dve.tensor_tensor(o, src, F8[:, :].unsqueeze(2).broadcast_to([P, HEADS, P]), ALU.add))
                        if kt == t:
                            link(dve.tensor_tensor(o, o, mask, ALU.add))
                    elif kt == t:
                        link(dve.tensor_tensor(o, src, mask, ALU.add))
                    else:
                        link(dve.tensor_copy(o, src))
                link(dve.tensor_reduce(peak[:, slot, :], dst[:, :, 0:(t + 1) * P], AX_X, ALU.max))
                dve.tensor_scalar(peak[:, slot, :], peak[:, slot, :], -scale, None, ALU.mult).then_inc(peak_ready, 1)

            def normalised(dst, src, slot, width):
                next_of(probs_ready, HEADS)
                link(dve.reciprocal(den[:, slot, :], den[:, slot, :]))
                link(dve.tensor_tensor(dst, src.rearrange("p (h c) -> p h c", h=HEADS),
                                       den[:, slot, :].unsqueeze(2).broadcast_to([P, HEADS, width]), ALU.mult))

            def angles():
                link(dve.tensor_copy(posf[:], posi[:]))
                for t in range(TILES):
                    link(dve.tensor_scalar(ang[:, t, :], cst[:, C_FREQ:C_FREQ + HALF], posf[:, t:t + 1], None, ALU.mult))
                magic = 1.5 * 2.0 ** 23
                link(dve.tensor_scalar(turns_n[:], ang[:], float(1 / (2 * np.pi)), magic, ALU.mult, ALU.add))
                link(dve.tensor_scalar(turns_n[:], turns_n[:], magic, None, ALU.subtract))
                rest = 2 * np.pi
                for bits in (6, 14, 22, None):
                    part = float(np.float32(rest)) if bits is None else float(np.floor(rest * 2.0 ** (bits - 0)) / 2.0 ** (bits - 0))
                    rest -= part
                    link(dve.scalar_tensor_tensor(out=ang[:].rearrange("p t c -> p (t c)"),
                                                  in0=turns_n[:].rearrange("p t c -> p (t c)"), scalar=-part,
                                                  in1=ang[:].rearrange("p t c -> p (t c)"), op0=ALU.mult, op1=ALU.add))
                lim = 3.1415925
                link(dve.tensor_scalar(ang[:], ang[:], lim, -lim, ALU.min, ALU.max))
                a2, n2 = ang[:].rearrange("p t c -> p (t c)"), turns_n[:].rearrange("p t c -> p (t c)")
                dve.scalar_tensor_tensor(out=n2, in0=a2, scalar=-1.0, in1=a2, op0=ALU.mult,
                                         op1=ALU.max).then_inc(angles_ready, 1)
                dve.wait_ge(angles_ready, 1)
                dve.tensor_scalar(n2, n2, -1.0, float(np.pi / 2), ALU.mult, ALU.add).then_inc(angles_ready, 1)

            def mix(s, turn):
                l, t = layer_tile(s)
                here = slice(t * P, (t + 1) * P)
                if s == 0:
                    for a in (qTf, qTs, FT):
                        dve.memset(a[:], 0.0).then_inc(zeroed, 1)
                    dve.wait_ge(zeroed, 3)
                    dve.wait_ge(consts_in, 80)
                    angles()
                if s == 1:
                    dve.wait_ge(late_in, 64)
                norm_rows(h[:, t, :])
                turn()
                copy_hT(gn[:, l, G_MIX:G_MIX + KT])
                for _ in range(4):
                    turn()
                wait_products(dve, "in", s)
                z = zf[:, 0, :]
                link(dve.tensor_tensor(z, bank[4][:, 256:260], fb[:, l, :], ALU.add))
                dve.scalar_tensor_tensor(out=zf[:, 1, :], in0=z, scalar=-1.0, in1=z, op0=ALU.mult,
                                         op1=ALU.max).then_inc(forget_in, 1)
                link(dve.tensor_copy(lat[:, 0:QR], bank[5][:, 256:512]))
                link(dve.tensor_copy(lat[:, QR:], bank[4][:, 260:388]))
                dve.tensor_copy(rot[:, HEADS, :], bank[4][:, 388:420]).then_inc(latents_left, 1)
                next_of(latents_left)
                next_of(forget_ln)
                dve.scalar_tensor_tensor(out=logf[:, t, :], in0=z, scalar=0.0, in1=zf[:, 2, :], op0=ALU.min,
                                         op1=ALU.subtract).then_inc(logf_ready, 1)
                squares(lat[:, 0:QR], 0, wa[:, 0:QR])
                squares(lat[:, QR:], 1, wa[:, QR:QR + KVR])
                rsqrt([QR, KVR])
                link(dve.tensor_scalar(lat[:, 0:QR], lat[:, 0:QR], inv[:, 1, 0:1], None, ALU.mult))
                dve.tensor_scalar(lat[:, QR:], lat[:, QR:], inv[:, 1, 1:2], None, ALU.mult).then_inc(normed, 1)
                turn()
                next_of(cum_ready)
                link(dve.tensor_scalar(F8[:], bank[0][:, 0:HEADS], 1.0 / FOX_SCALE, None, ALU.mult))
                link(dve.tensor_copy(FT[0:HEADS, here], bank[0][0:HEADS, P:2 * P]))
                dve.tensor_tensor(latT[:], bank[1][:, 0:384].rearrange("p (k c) -> p k c", k=3),
                                  gn[:, l, G_Q:G_Q + 3].unsqueeze(2).broadcast_to([P, 3, P]),
                                  ALU.mult).then_inc(latT_ready, 1)
                turn()
                wait_products(dve, "latent", s)
                q3 = bank[2][:, 0:384].rearrange("p (h c) -> p h c", h=HEADS)
                link(dve.tensor_copy(rot[:, 0:HEADS, :], q3[:, :, NOPE:QK]))
                link(dve.tensor_copy(qf[:, :, 0:NOPE], q3[:, :, 0:NOPE]))
                if s == 0:
                    dve.wait_ge(trig_ready, 2)
                x1, x2 = rot[:, :, 0:HALF], rot[:, :, HALF:ROPE]
                c_, s_ = (a[:, t, :].unsqueeze(1).broadcast_to([P, HEADS + 1, HALF]) for a in (cos, sin))
                for i, (a, b) in enumerate(((x1, c_), (x2, s_), (x1, s_), (x2, c_))):
                    ins = dve.tensor_tensor(rot_p[:, i], a, b, ALU.mult)
                    link(ins)
                link(dve.tensor_tensor(rotated[:, :, 0:HALF], rot_p[:, 0], rot_p[:, 1], ALU.subtract))
                link(dve.tensor_tensor(rotated[:, :, HALF:ROPE], rot_p[:, 2], rot_p[:, 3], ALU.add))
                link(dve.tensor_copy(qf[:, :, NOPE:QK], rotated[:, 0:HEADS, :]))
                dve.tensor_copy(kf[:, :, NOPE:QK],
                                rotated[:, HEADS:HEADS + 1, :].broadcast_to([P, HEADS, ROPE])).then_inc(rotated_ready, 1)
                turn()
                peaks(s, fox_s, 0, FOX_SCALE, True)
                turn()
                next_of(soft_ready, t + 1)
                for kt in range(t + 1):
                    b = bank[kt][:, :]
                    link(dve.tensor_scalar(logb[:, kt, :], b, FOX_SCALE, 0.0, ALU.mult, ALU.min))
                    link(dve.tensor_tensor(logb[:, kt, :], logb[:, kt, :], soft[:, kt, :], ALU.subtract))
                    ins = dve.scalar_tensor_tensor(out=lom[:, kt, :], in0=b, scalar=-FOX_SCALE, in1=logb[:, kt, :],
                                                   op0=ALU.mult, op1=ALU.add)
                    if kt < t:
                        link(ins)
                link(ins)
                strict4 = strict.unsqueeze(1).broadcast_to([P, HEADS, P])
                lom3 = lom[:, t, :].rearrange("p (h q) -> p h q", h=HEADS)
                dve.tensor_tensor(lom3, lom3, strict4, ALU.mult).then_inc(lom_ready, 1)
                turn()
                next_of(attended)
                normalised(y[:, 0:256].rearrange("p (h c) -> p h c", h=HEADS), bank[4][:, 0:256], 0, HD)
                next_of(rest_ready)
                for kt in range(t + 1):
                    ins = dve.tensor_tensor(logb[:, kt, :], logb[:, kt, :], bank[2 + kt][:, :], ALU.add)
                    if kt < t:
                        link(ins)
                ins.then_inc(stick_sum, 1)
                next_of(stick_exp, t + 1)
                soft3 = soft[:, t, :].rearrange("p (h q) -> p h q", h=HEADS)
                dve.tensor_tensor(soft3, soft3, strict4, ALU.mult).then_inc(stick_ready, 1)
                turn()
                next_of(attended)
                link(dve.tensor_copy(y[:, 256:512], bank[4][:, 256:512]))
                peaks(s, mla_s, 1, MLA_SCALE, False)
                turn()
                turn()
                next_of(attended)
                normalised(y[:, 512:1024].rearrange("p (h c) -> p h c", h=HEADS), bank[5][:, :], 1, VD)
                bounds = ((0, 256), (256, 512), (512, 1024))
                for i, (a, b) in enumerate(bounds):
                    squares(y[:, a:b], i, rows_n[:, a:b])
                rsqrt([b - a for a, b in bounds])
                for i, (a, b) in enumerate(bounds):
                    ins = dve.tensor_scalar(rows_n[:, a:b], y[:, a:b], inv[:, 1, i:i + 1], None, ALU.mult)
                    if i < 2:
                        link(ins)
                ins.then_inc(normed, 1)
                turn()
                copy_hT(gn[:, l, G_OUT:G_OUT + KT])
                turn()
                turn()
                wait_products(dve, "out", s)
                for c in range(2):
                    part = h[:, t, c * 512:(c + 1) * 512]
                    link(dve.tensor_tensor(part, part, bank[2 + c][:, :], ALU.add))
                if s == 0:
                    dve.wait_ge(late_in, 64)
                squares(h[:, t, :], 0, rows_n[:, :])
                rsqrt([D])
                dve.scalar_tensor_tensor(out=xc[:, s % 2, :], in0=h[:, t, :], scalar=inv[:, 1, 0:1],
                                         in1=gffn[:, l, :], op0=ALU.mult, op1=ALU.mult).then_inc(normed, 1)
                turn()
                copy_hT(None)
                turn()
                turn()
                turn()
                choose(s, turn)

            def top16(n, values, indices, data, spare, width, done_first):
                for i in range(n):
                    ins = dve.max(out=values[:, i, 0:8], in_=data(i))
                link(ins)
                for i in range(n):
                    ins = dve.max_index(out=indices[:, i, 0:8], in_max=values[:, i, 0:8], in_values=data(i))
                link(ins)
                for i in range(n):
                    ins = dve.match_replace(out=spare(i), in_to_replace=values[:, i, 0:8], in_values=data(i),
                                            imm_value=-3e38)
                link(ins)
                done_first()
                for i in range(n):
                    ins = dve.max(out=values[:, i, 8:16], in_=spare(i))
                link(ins)
                for i in range(n):
                    ins = dve.max_index(out=indices[:, i, 8:16], in_max=values[:, i, 8:16], in_values=spare(i))
                link(ins)

            def choose(s, turn):
                l, t = layer_tile(s)
                wait_products(dve, "keys", s)
                top16(2 * PH, top_v, top_i, score, lambda i: wb[:, i * P:(i + 1) * P], P, turn)
                turn()
                link(dve.tensor_copy(top_f[:], top_i[:]))
                pairs = wa[:].rearrange("p (h a b) -> p h a b", h=PH, a=TOPK)
                first = top_v[:].rearrange("p (h two) a -> p h two a", two=2)[:, :, 0, :]
                second = top_v[:].rearrange("p (h two) a -> p h two a", two=2)[:, :, 1, :]
                link(dve.tensor_tensor(pairs, first.unsqueeze(3).broadcast_to([P, PH, TOPK, TOPK]),
                                       second.unsqueeze(2).broadcast_to([P, PH, TOPK, TOPK]), ALU.add))
                top16(PH, best_v, best_i, lambda i: wa[:, i * 256:(i + 1) * 256],
                      lambda i: wb[:, i * 256:(i + 1) * 256], 256, turn)
                link(dve.tensor_scalar(part_i[:, 0], best_i[:], 4, None, ALU.logical_shift_right))
                link(dve.tensor_scalar(part_i[:, 1], best_i[:], 15, None, ALU.bitwise_and))
                link(dve.tensor_copy(part_f[:], part_i[:]))
                link(dve.tensor_copy(gsum[:, 0, :], best_v[:, :, 0]))
                dve.tensor_tensor(best_v[:], best_v[:], gsum[:, 0, :].unsqueeze(2).broadcast_to([P, PH, TOPK]),
                                  ALU.subtract).then_inc(gate_in, 1)
                turn()
                for half, work in ((0, wa), (1, wb)):
                    w4 = work[:].rearrange("p (h k a) -> p h k a", h=PH, k=TOPK)
                    names = top_f[:].rearrange("p (h two) a -> p h two a", two=2)[:, :, half, :]
                    iota4 = iota.unsqueeze(1).broadcast_to([P, PAIRS, TOPK]).rearrange("p (h k) a -> p h k a", h=PH)
                    link(dve.tensor_tensor(w4, part_f[:, half].unsqueeze(3).broadcast_to([P, PH, TOPK, TOPK]), iota4,
                                           ALU.is_equal))
                    link(dve.tensor_tensor(w4, w4, names.unsqueeze(2).broadcast_to([P, PH, TOPK, TOPK]), ALU.mult))
                    link(dve.tensor_reduce(part_id[:, half], w4, AX_X, ALU.add))
                    turn()
                a, b = (part_id[:, i].rearrange("p h k -> p (h k)") for i in range(2))
                link(dve.scalar_tensor_tensor(out=a, in0=a, scalar=float(NKEY), in1=b, op0=ALU.mult, op1=ALU.add))
                dve.tensor_scalar(ids[:, s % 2, :], a, float(l * EXPERTS), None, ALU.add).then_inc(ids_ready, 1)
                next_of(gate_exp)
                link(dve.tensor_reduce(gsum[:, 1, :], best_v[:], AX_X, ALU.add))
                link(dve.reciprocal(gsum[:, 1, :], gsum[:, 1, :]))
                dve.tensor_tensor(gate[:, s % 2, :].rearrange("p (h k) -> p h k", h=PH), best_v[:],
                                  gsum[:, 1, :].unsqueeze(2).broadcast_to([P, PH, TOPK]),
                                  ALU.mult).then_inc(gate_ready, 1)

            def begin(w):
                if w == 0:
                    return
                dve.wait_ge(row_used, w * PAIRS)
                for c in range(2):
                    dve.tensor_copy(h[:, (w - 1) % 2, c * 512:(c + 1) * 512], acc[:, c, :]).then_inc(acc_read, 1)
                dve.wait_ge(acc_read, 2 * w)

            def embed(s, turn):
                l, t = layer_tile(s)
                norm_rows(h[:, t, :])
                turn()
                copy_hT(gn[:, l, G_PLE:G_PLE + KT])
                turn()
                turn()
                next_of(sig_ready, 2)
                for c in range(2):
                    g = gate_s[:, c * 512:(c + 1) * 512]
                    part = h[:, t, c * 512:(c + 1) * 512]
                    link(dve.tensor_tensor(g, g, bank[4 + c][:, :], ALU.mult))
                    link(dve.tensor_tensor(part, part, g, ALU.add))

            def finish(t):
                dst = (y, rows_n)[t]
                squares(h[:, t, :], 0, dst[:, :])
                rsqrt([D])
                dve.scalar_tensor_tensor(out=dst[:, :], in0=h[:, t, :], scalar=inv[:, 1, 0:1], in1=gfin[:],
                                         op0=ALU.mult, op1=ALU.mult).then_inc(result_ready, 1)

            walk(Stream(dve, experts), mix, embed, finish, begin)


def constants():
    c = np.zeros((P, C_W), np.float32)
    i = np.arange(P)
    c[:, C_ID:C_ID + P] = np.eye(P)
    c[:, C_LE:C_LE + P] = i[:, None] <= i[None, :]
    c[:, C_GT:C_GT + P] = i[:, None] > i[None, :]
    c[:, C_ONE:C_ONE + P] = 1.0
    c[:, C_CAUSAL:C_CAUSAL + P] = np.where(i[None, :] <= i[:, None], 0.0, NEG)
    c[:, C_STRICT:C_STRICT + P] = i[:, None] < i[None, :]
    for hd in range(HEADS):
        c[hd, C_SEL + hd * P:C_SEL + (hd + 1) * P] = -1.0 / FOX_SCALE
    c[:, C_FREQ:C_FREQ + HALF] = np.float32(10000.0) ** (-np.arange(HALF, dtype=np.float32) / np.float32(HALF))
    c[:, C_IOTA:C_IOTA + TOPK] = np.arange(TOPK)
    return c


def kernel(x, p, positions, norm_mix_g, w_in, b_forget, mla_q_norm_g, w_uq, mla_kv_norm_g, w_ukv,
           mix_out_norm_g, w_o, norm_ffn_g, peer_w_query, peer_sub_keys, peer_u, peer_v,
           w_ple, ple_norm_g, w_ple_gate, final_norm_g):
    import concourse.bacc as bacc
    from concourse.bass_utils import run_bass_kernel_spmd as run

    def slabs(g):
        g = np.asarray(g)
        return g.reshape(DEPTH, -1, P)

    gains = np.concatenate([slabs(norm_mix_g), slabs(mla_q_norm_g), slabs(mla_kv_norm_g),
                            slabs(mix_out_norm_g), slabs(ple_norm_g)], axis=1)
    uq = np.asarray(w_uq).reshape(DEPTH, 2, P, -1).transpose(0, 2, 1, 3).reshape(DEPTH, P, -1)
    arrays = {
        "x": np.asarray(x).reshape(SEQ, D),
        "p_t": np.asarray(p).reshape(DEPTH, SEQ, 256).transpose(0, 2, 1).reshape(DEPTH * 256, SEQ),
        "pos": np.asarray(positions).reshape(TILES, P).T,
        "gains": gains.transpose(2, 0, 1),
        "forget_b": np.asarray(b_forget),
        "ffn_g": np.asarray(norm_ffn_g),
        "final_g": np.asarray(final_norm_g),
        "w_in": np.asarray(w_in),
        "w_latent": np.concatenate([uq, np.asarray(w_ukv)], axis=2),
        "w_out": np.asarray(w_o),
        "w_query": np.asarray(peer_w_query),
        "keys": np.asarray(peer_sub_keys).transpose(0, 2, 4, 1, 3).reshape(DEPTH, P, PH * NKEY),
        "rows": np.concatenate([np.asarray(peer_u), np.asarray(peer_v)], axis=2).reshape(DEPTH * EXPERTS, 2 * D),
        "w_ple": np.asarray(w_ple),
        "w_gate": np.asarray(w_ple_gate),
        "consts": constants(),
    }
    nc = bacc.Bacc("TRN2", target_bir_lowering=False, num_devices=1)
    aps, feed = {}, {}
    for name, a in arrays.items():
        a = np.ascontiguousarray(a)
        feed["in_" + name] = a
        aps[name] = nc.dram_tensor("in_" + name, a.shape, mybir.dt.from_np(a.dtype), kind="ExternalInput").ap()
    out = nc.dram_tensor("out", (SEQ, D), F32, kind="ExternalOutput").ap()
    trunk(nc, out=out, **aps)
    result = run(nc, [feed], core_ids=[0])
    return result.results[0]["out"].reshape(1, SEQ, D)
```

```python
from contextlib import ExitStack

import numpy as np
import concourse.bass as bass
from concourse import mybir

ALU = mybir.AluOpType
ACT = mybir.ActivationFunctionType
AX_X = mybir.AxisListType.X
F32 = mybir.dt.float32
I32 = mybir.dt.int32
U32 = mybir.dt.uint32

P = 128
D = 1024
KT = D // P
SEQ, TILES, DEPTH = 256, 2, 2
STEPS = DEPTH * TILES
HEADS, HD = 4, 64
NOPE, ROPE, VD = 64, 32, 128
QK = NOPE + ROPE
QR, KVR = 256, 128
FOX_SCALE, MLA_SCALE = HD ** -0.5, QK ** -0.5
IN_W = 3 * 256 + 4 + 3 * 256 + QR + KVR + ROPE
EPS = 1e-6
PH, NKEY, TOPK = 8, 128, 16
EXPERTS = NKEY * NKEY
PAIRS = PH * TOPK
RING, GROUP = 8, 4
GROUPS = PAIRS // GROUP
WRING, WSLOT = 4, 2048
NEG = -1e30
HALF = ROPE // 2
C_ID, C_LE, C_GT, C_ONE, C_CAUSAL, C_STRICT, C_SEL, C_FREQ, C_IOTA = 0, 128, 256, 384, 512, 640, 768, 1280, 1296
C_W = 1312
G_MIX, G_Q, G_KV, G_OUT, G_PLE, G_W = 0, 8, 10, 11, 19, 27

IN_LOADS = [("in", k) for k in range(KT)]
REST_LOADS = [("latent", 0)] + [("out", k) for k in range(KT // 2)] + \
             [("query", k) for k in range(KT // 2)] + [("keys", 0)]
EMBED_LOADS = [("ple", 0)] + [("gate", k) for k in range(KT // 2)]
CHUNKS, CHUNK_HEADS = 4, PH // 4
CHUNK_PAIRS = CHUNK_HEADS * TOPK


def layer_tile(s):
    return s // TILES, s % TILES


def weight_order():
    order = [(kind, k, 0) for kind, k in REST_LOADS]
    for w in range(STEPS):
        if w >= 1:
            order += [(kind, k, w - 1) for kind, k in EMBED_LOADS]
        if w + 1 < STEPS:
            order += [(kind, k, w + 1) for kind, k in (IN_LOADS if w >= 1 else []) + REST_LOADS]
    return order + [(kind, k, STEPS - 1) for kind, k in EMBED_LOADS]


FRONT = [1] + [.5] * KT
LEAVE = [1]
REST = [1, 1, 1, 1, 1, 1, 1, 1] + [.5] * (KT // 2) + [1] + [.5] * (KT // 2)
CHOOSE = [1, 1]
EMBED = [1] + [.5] * 4


def window_turns(w):
    turns = CHOOSE * (CHUNKS - 1) if w == 0 else EMBED
    if w + 1 < STEPS:
        return turns + (FRONT + LEAVE if w >= 1 else []) + REST + CHOOSE * CHUNKS + [1]
    return turns + [1, 3]


class Shares:

    def __init__(self, stream, step):
        self.stream, self.step, self.turns, self.n, self.sent = stream, step, window_turns(step), 0, 0

    def __call__(self):
        self.n += 1
        assert self.n <= len(self.turns)
        a, b = self.sent, round(GROUPS * sum(self.turns[:self.n]) / sum(self.turns))
        self.sent = b
        if self.n == len(self.turns) and self.step == STEPS - 1:
            self.stream(self.step, a, b - 1)
            self.stream.last(self.step, b - 1)
        else:
            self.stream(self.step, a, b)


def share_out(stream, step, a, b):
    if a % 2 and a < b:
        stream.group(step, a // 2, 1)
        a += 1
    if b - a >= 4:
        stream.loop(step, a // 2, b // 2)
        a = b // 2 * 2
    while a < b:
        stream.group(step, a // 2, a % 2)
        a += 1


class Stream:

    def __init__(self, eng, body):
        self.eng, self.body = eng, body

    def group(self, step, i, half):
        self.body(step, i, half)

    def loop(self, step, lo, hi):
        with self.eng.Fori(lo, hi) as i:
            for half in range(2):
                self.body(step, i, half)

    def last(self, step, g):
        self.body(step, g // 2, g % 2, 1)

    def __call__(self, step, a, b):
        share_out(self, step, a, b)


def walk(stream, parts):
    def nothing():
        pass

    ahead = parts["ahead"]
    parts["front"](0, ahead)
    parts["leave"](0, ahead)
    parts["rest"](0, ahead)
    parts["choose"](0, 0, ahead)
    parts["leave"](1, nothing)
    for w in range(STEPS):
        parts["begin"](w)
        turn = Shares(stream, w)
        if w == 0:
            for c in range(1, CHUNKS):
                parts["choose"](0, c, turn)
        if w >= 1:
            parts["lift"](w - 1)
            parts["embed"](w - 1, turn)
        if w + 1 < STEPS:
            if w >= 1:
                parts["front"](w + 1, turn)
                parts["leave"](w + 1, turn)
            parts["rest"](w + 1, turn)
            for c in range(CHUNKS):
                parts["choose"](w + 1, c, turn)
        else:
            parts["finish"](0)
            turn()
            parts["lift"](w)
        assert turn.n == len(turn.turns) - 1
        turn()
    parts["begin"](STEPS)
    parts["embed"](STEPS - 1, nothing)
    parts["finish"](1)


def trunk(nc, x, p_t, pos, gains, forget_b, ffn_g, final_g, w_in, w_latent, w_out, w_query, keys,
          rows, w_ple, w_gate, consts, out):
    with ExitStack() as ctx:
        def sb(name, shape, dt=F32):
            return ctx.enter_context(nc.sbuf_tensor(name, shape, dt))

        def sem(name):
            return ctx.enter_context(nc.semaphore(name))

        ring = sb("ring", [P, RING, 2 * D])
        wring = sb("wring", [P, WRING, WSLOT])
        h = sb("h", [P, TILES, D])
        rows_n = sb("rows_n", [P, D])
        hT = sb("hT", [P, KT, P])
        y = sb("y", [P, D])
        xc = sb("xc", [P, 2, D])
        wa = sb("wa", [P, 2048])
        wb = sb("wb", [P, 2048])
        cst = sb("cst", [P, C_W])
        gn = sb("gn", [P, DEPTH, G_W])
        fb = sb("fb", [P, DEPTH, HEADS])
        gffn = sb("gffn", [P, DEPTH, D])
        gfin = sb("gfin", [P, D])
        pT = sb("pT", [P, DEPTH * 2, SEQ])
        posi = sb("posi", [P, TILES], I32)
        posf = sb("posf", [P, TILES])
        ang = sb("ang", [P, TILES, HALF])
        turns_n = sb("turns_n", [P, TILES, HALF])
        sin = sb("sin", [P, TILES, HALF])
        cos = sb("cos", [P, TILES, HALF])
        qTf = sb("qTf", [P, HEADS, P])
        kTf = sb("kTf", [P, 2, SEQ])
        qTs = sb("qTs", [P, HEADS, P])
        kTs = sb("kTs", [P, 2, SEQ])
        vf = sb("vf", [P, TILES, 256])
        vs = sb("vs", [P, TILES, 256])
        qTm = sb("qTm", [P, HEADS, P])
        kTm = sb("kTm", [P, HEADS, SEQ])
        vm = sb("vm", [P, TILES, HEADS, VD])
        zf = sb("zf", [P, 3, HEADS])
        logf = sb("logf", [P, TILES, HEADS])
        F8 = sb("F8", [P, HEADS])
        FT = sb("FT", [P, SEQ])
        lat = sb("lat", [P, QR + KVR])
        latT = sb("latT", [P, 3, P])
        qf = sb("qf", [P, HEADS, QK])
        kf = sb("kf", [P, HEADS, QK])
        rot = sb("rot", [P, HEADS + 1, ROPE])
        rot_p = sb("rot_p", [P, 4, HEADS + 1, HALF])
        rotated = sb("rotated", [P, HEADS + 1, ROPE])
        peak = sb("peak", [P, 2, HEADS])
        den = sb("den", [P, 2, HEADS])
        ffn_r = sb("ffn_r", [P, 2])
        ssq = sb("ssq", [P, 3])
        inv = sb("inv", [P, 4, 3])
        top_v = sb("top_v", [P, 2 * PH, TOPK])
        top_i = sb("top_i", [P, 2 * PH, TOPK], U32)
        top_f = sb("top_f", [P, 2 * PH, TOPK])
        best_v = sb("best_v", [P, PH, TOPK])
        best_i = sb("best_i", [P, PH, TOPK], U32)
        part_i = sb("part_i", [P, 2, PH, TOPK], U32)
        part_f = sb("part_f", [P, 2, PH, TOPK])
        part_id = sb("part_id", [P, 2, PH, TOPK])
        gsum = sb("gsum", [P, 2, PH])
        gate = sb("gate", [P, 2, PAIRS])
        ids = sb("ids", [P, 2, PAIRS], I32)
        table_spare = sb("table_spare", [P, 1])
        pre = sb("pre", [P, RING])
        gel = sb("gel", [P, RING])
        act_w = sb("act_w", [P, RING])
        diag = sb("diag", [P, RING, P])

        acc = ctx.enter_context(nc.psum_tensor("acc", [P, 2, 512], F32))
        bank = [ctx.enter_context(nc.psum_tensor(f"bank{i}", [P, 512], F32)) for i in range(6)]

        ident = cst[:, C_ID:C_ID + P]
        tri_le = cst[:, C_LE:C_LE + P]
        tri_gt = cst[:, C_GT:C_GT + P]
        ones = cst[:, C_ONE:C_ONE + P]
        causal = cst[:, C_CAUSAL:C_CAUSAL + P]
        strict = cst[:, C_STRICT:C_STRICT + P]
        iota = cst[:, C_IOTA:C_IOTA + TOPK]
        fox_s = wa[:, 0:1024].rearrange("p (h k) -> p h k", h=HEADS)
        probsT = wa[:, 1024:2048].rearrange("p (t c) -> p t c", t=2)
        soft = wa[:, 0:1024].rearrange("p (t c) -> p t c", t=2)
        logb = wb[:, 0:1024].rearrange("p (t c) -> p t c", t=2)
        lom = wb[:, 1024:2048].rearrange("p (t c) -> p t c", t=2)
        mla_s = wb[:, 0:1024].rearrange("p (h k) -> p h k", h=HEADS)
        gate_s = wb[:, 0:1024]
        hT_next = xc[:, 1, :].rearrange("p (k c) -> p k c", k=KT)
        queryT = y[:, :].rearrange("p (h c) -> p h c", h=PH)

        def score(hp):
            hd, half = divmod(hp, 2)
            return bank[4 * half + hd // 4][:, hd % 4 * P:hd % 4 * P + P]

        x_in = [sem(f"x_in{t}") for t in range(TILES)]
        consts_in = sem("consts_in")
        small_in = sem("small_in")
        late_in = sem("late_in")
        weight_in = [sem(f"weight_in{i}") for i in range(WRING)]
        weight_used = sem("weight_used")
        row_in = [sem(f"row_in{i}") for i in range(RING)]
        dotted = sem("dotted")
        gelued = sem("gelued")
        weighted = sem("weighted")
        diag_ready = sem("diag_ready")
        row_used = sem("row_used")
        acc_read = sem("acc_read")
        ids_ready = sem("ids_ready")
        gate_ready = sem("gate_ready")
        dve_done = sem("dve_done")
        act_done = sem("act_done")
        zeroed = sem("zeroed")
        angles_ready = sem("angles_ready")
        trig_ready = sem("trig_ready")
        normed = sem("normed")
        turned = sem("turned")
        hT_ready = sem("hT_ready")
        projected = sem("projected")
        ahead_heads = sem("ahead_heads")
        cum_copied = sem("cum_copied")
        slab_in = [sem(f"slab_in{k}") for k in range(KT)]
        slab_used = sem("slab_used")
        latent_r = sem("latent_r")
        ple_r = sem("ple_r")
        heads_ready = sem("heads_ready")
        forget_in = sem("forget_in")
        forget_ln = sem("forget_ln")
        latents_left = sem("latents_left")
        logf_ready = sem("logf_ready")
        cum_ready = sem("cum_ready")
        latent_turned = sem("latent_turned")
        latT_ready = sem("latT_ready")
        latent_copied = sem("latent_copied")
        rotated_ready = sem("rotated_ready")
        full_turned = sem("full_turned")
        full_ready = sem("full_ready")
        scored = sem("scored")
        peak_ready = sem("peak_ready")
        probs_ready = sem("probs_ready")
        probs_turned = sem("probs_turned")
        probsT_ready = sem("probsT_ready")
        stick_scored = sem("stick_scored")
        soft_ready = sem("soft_ready")
        lom_ready = sem("lom_ready")
        rest_ready = sem("rest_ready")
        stick_sum = sem("stick_sum")
        stick_exp = sem("stick_exp")
        stick_ready = sem("stick_ready")
        attended = sem("attended")
        query_ready = sem("query_ready")
        gate_in = sem("gate_in")
        gate_exp = sem("gate_exp")
        gate_half = sem("gate_half")
        sig_ready = sem("sig_ready")
        result_ready = sem("result_ready")
        stored = sem("stored")

        def leave_banks(s):
            return (bank[2], bank[3]) if s == 1 else (bank[0], bank[1])

        order = weight_order()
        block = ctx.enter_context(nc.Block())

        def wait_products(eng, kind, s, last=KT):
            eng.wait_ge(weight_used, 1 + max(n for n, (a, k, b) in enumerate(order) if (a, b) == (kind, s) and k <= last))

        def front_banks(s):
            return [acc[:, 0, :], acc[:, 1, :], acc[:, 0, :], acc[:, 1, :]] if s == 1 else [b[:, :] for b in bank[2:6]]

        def waiter(eng):
            seen = {}

            def next_of(s, n=1):
                seen[s.name] = seen.get(s.name, 0) + n
                eng.wait_ge(s, seen[s.name])
            return next_of

        @block.sync
        def _(sp):
            def load(dst, src, s):
                sp.dma_start(dst, src).then_inc(s, 16)

            load(h[:, 0, :], x[0:P, :], x_in[0])
            load(cst[:], consts, consts_in)
            load(gn[:], gains, consts_in)
            load(fb[:], forget_b.partition_broadcast(P), small_in)
            load(posi[:], pos, small_in)
            for k in range(KT):
                load(ring[:, k, 0:IN_W], w_in[0, k * P:(k + 1) * P, :], slab_in[k])
                if k == 1:
                    load(h[:, 1, :], x[P:2 * P, :], x_in[1])
            source = {
                "in": lambda l, k: w_in[l, k * P:(k + 1) * P, :],
                "latent": lambda l, k: w_latent[l],
                "out": lambda l, k: w_out[l, 2 * k * P:2 * (k + 1) * P, :].rearrange("(a p) n -> p a n", p=P),
                "query": lambda l, k: w_query[l, 2 * k * P:2 * (k + 1) * P, :].rearrange("(a p) n -> p a n", p=P),
                "gate": lambda l, k: w_gate[l, 2 * k * P:2 * (k + 1) * P, :].rearrange("(a p) n -> p a n", p=P),
                "ple": lambda l, k: w_ple[l].rearrange("(a p) n -> p a n", p=P),
                "keys": lambda l, k: keys[l],
            }
            for n, (kind, k, s) in enumerate(order):
                if n >= WRING:
                    sp.wait_ge(weight_used, n - WRING + 1)
                src = source[kind](layer_tile(s)[0], k)
                if len(src.shape) == 3:
                    dst = wring[:, n % WRING, :].rearrange("p (a n) -> p a n", a=2)
                else:
                    dst = wring[:, n % WRING, 0:src.shape[1]]
                sp.dma_start(dst, src).then_inc(weight_in[n % WRING], 16)
                if n == WRING - 1:
                    load(gffn[:], ffn_g.partition_broadcast(P), late_in)
                    load(gfin[:], final_g.partition_broadcast(P), late_in)
                    load(pT[:], p_t.rearrange("(a p) s -> p a s", p=P), late_in)
            for t in range(TILES):
                sp.wait_ge(result_ready, t + 1)
                sp.dma_start(out[t * P:(t + 1) * P, :], (y, rows_n)[t][:, :]).then_inc(stored, 16)
            sp.wait_ge(stored, 16 * TILES)

        @block.gpsimd
        def _(pool):
            for n in range(STEPS * PAIRS):
                w, k = divmod(n, PAIRS)
                if k % CHUNK_PAIRS == 0:
                    pool.wait_ge(ids_ready, n // CHUNK_PAIRS + 1)
                if n < RING:
                    pool.wait_ge(slab_used, n + 1)
                else:
                    pool.wait_ge(row_used, n - RING + 1)
                pool.indirect_dma_start(
                    out=ring[:, n % RING, :], out_offset=None, in_=rows,
                    in_offset=bass.IndirectOffsetOnAxis(ap=ids[:, w % 2, k:k + 1], axis=0),
                ).then_inc(row_in[n % RING], 16)

        @block.tensor
        def _(pe):
            next_of = waiter(pe)
            used = [0]

            def weights(ahead_by=0):
                n = used[0] + ahead_by
                pe.wait_ge(weight_in[n % WRING], 16 * (n // WRING + 1))
                return wring[:, n % WRING, :]

            def release(last):
                used[0] += 1
                last.then_inc(weight_used, 1)

            def experts(step, i, half, unit=GROUP):
                for j in range(half * GROUP, half * GROUP + GROUP):
                    pe.wait_ge(diag_ready, step * PAIRS + i * RING + j + 1)
                    for c in range(2):
                        last = pe.matmul(acc[:, c, :], diag[:, j, :], ring[:, j, D + c * 512:D + c * 512 + 512],
                                         start=False, stop=True, skip_group_check=True)
                    last.then_inc(row_used, 1)

            def begin(w):
                if w == STEPS:
                    return
                if w >= 1:
                    pe.wait_ge(acc_read, 2 * w)
                else:
                    next_of(heads_ready, 2)
                for c in range(2):
                    pe.matmul(acc[:, c, :], ident, h[:, w % 2, c * 512:c * 512 + 512],
                              start=True, stop=True, skip_group_check=True)

            def turn_rows(src):
                for k in range(KT):
                    last = pe.transpose(bank[k // 4][:, k % 4 * P:k % 4 * P + P], src[:, k * P:(k + 1) * P], ident)
                last.then_inc(turned, 1)

            def project(s, part, k, w, hT_s):
                b = front_banks(s)
                a, z = k == 0, k == KT - 1
                if part == 0:
                    for i in range(2):
                        for col in range(4):
                            c0 = 772 * i + col * P
                            last = pe.matmul(b[i][:, col * P:(col + 1) * P], w[:, c0:c0 + P], hT_s[:, k, :],
                                             start=(a and col == 0), stop=z, skip_group_check=True)
                else:
                    pe.matmul(b[2][:, 0:260], hT_s[:, k, :], w[:, 512:772], start=a, stop=z, skip_group_check=True)
                    pe.matmul(b[2][:, 260:420], hT_s[:, k, :], w[:, 1796:1956], start=False, stop=z, skip_group_check=True)
                    last = pe.matmul(b[3][:, :], hT_s[:, k, :], w[:, 1284:1796], start=a, stop=z, skip_group_check=True)
                return last

            def head_scores(s, qT, kT, width, fox):
                l, t = layer_tile(s)
                for kt in range(t + 1):
                    for hd in range(HEADS):
                        o = bank[kt][:, hd * P:(hd + 1) * P]
                        keys_at = slice(kt * P, (kt + 1) * P)
                        if fox:
                            pe.matmul(o, qT[:, hd, :], kT[:, hd // 2, keys_at], start=True, stop=False)
                            last = pe.matmul(o, cst[:, C_SEL + hd * P:C_SEL + (hd + 1) * P], FT[:, keys_at],
                                             start=False, stop=True)
                        else:
                            last = pe.matmul(o, qT[0:width, hd, :], kT[0:width, hd, keys_at], start=True, stop=True)
                last.then_inc(scored, 1)

            def turn_probs(s, src):
                l, t = layer_tile(s)
                next_of(probs_ready, HEADS)
                for kt in range(t + 1):
                    for hd in range(HEADS):
                        last = pe.transpose(bank[2 + kt][:, hd * P:(hd + 1) * P], src[:, hd, kt * P:(kt + 1) * P], ident)
                last.then_inc(probs_turned, 1)

            def weigh(s, dst, src, v, width):
                l, t = layer_tile(s)
                for hd in range(HEADS):
                    for kt in range(t + 1):
                        last = pe.matmul(dst[:, hd * width:(hd + 1) * width], src[:, kt, hd * P:(hd + 1) * P],
                                         v(kt, hd), start=(kt == 0), stop=(kt == t))
                last.then_inc(attended, 1)

            def front(s, turn):
                if s == 0:
                    pe.wait_ge(consts_in, 32)
                next_of(normed)
                turn_rows(rows_n)
                turn()
                next_of(hT_ready, 2)
                for k in range(KT):
                    if s == 0:
                        pe.wait_ge(slab_in[k], 16)
                        w = ring[:, k, :]
                    else:
                        w = weights()
                    project(s, 0, k, w, hT)
                    last = project(s, 1, k, w, hT)
                    if s >= 1:
                        release(last)
                    elif k == KT - 1:
                        last.then_inc(projected, 1)
                    turn()

            ahead_turn = [0]

            def ahead():
                n = ahead_turn[0]
                ahead_turn[0] += 1
                if n == 3:
                    next_of(normed)
                    turn_rows(rows_n)
                first = {9: (0, 2), 10: (2, 3), 11: (3, 5), 12: (5, 6), 13: (6, 7), 14: (7, 8)}.get(n, (0, 0))
                second = {27: (0, 8)}.get(n, (0, 0))
                if n == 9:
                    next_of(hT_ready, 2)
                for k in range(*first):
                    last = project(1, 0, k, ring[:, k, :], hT_next)
                    if k == KT - 1:
                        last.then_inc(ahead_heads, 1)
                if n == 27:
                    next_of(heads_ready, 6)
                for k in range(*second):
                    project(1, 1, k, ring[:, k, :], hT_next).then_inc(slab_used, 1)

            def leave(s, turn):
                l, t = layer_tile(s)
                cum, turned_lat = leave_banks(s)
                next_of(normed)
                for k in range(3):
                    last = pe.transpose(turned_lat[:, k * P:(k + 1) * P], lat[:, k * P:(k + 1) * P], ident)
                last.then_inc(latent_turned, 1)
                if s == 0:
                    turn()
                next_of(logf_ready)
                pe.matmul(cum[:, 0:HEADS], tri_le, logf[:, t, :], start=True, stop=(t == 0))
                if t:
                    pe.matmul(cum[:, 0:HEADS], ones, logf[:, 0, :], start=False, stop=True)
                last = pe.matmul(cum[0:HEADS, P:2 * P], logf[:, t, :], tri_le, start=True, stop=(t == 0))
                if t:
                    last = pe.matmul(cum[0:HEADS, P:2 * P], logf[:, 0, :], ones, start=False, stop=True)
                last.then_inc(cum_ready, 1)
                if s > 0:
                    turn()

            def rest(s, turn):
                l, t = layer_tile(s)
                next_of(latT_ready)
                next_of(cum_copied)
                if s != 1:
                    next_of(heads_ready, 8)
                w = weights()
                for k in range(2):
                    pe.matmul(bank[2][:, 0:384], latT[:, k, :], w[:, k * 384:(k + 1) * 384], start=(k == 0), stop=(k == 1))
                for c in range(2):
                    last = pe.matmul(bank[3 + c][:, 0:384], latT[:, 2, :], w[:, 768 + c * 384:768 + (c + 1) * 384],
                                     start=True, stop=True)
                release(last)
                turn()
                head_scores(s, qTf, kTf, HD, True)
                next_of(rotated_ready)
                next_of(latent_copied, 4)
                for b, src in ((4, qf), (5, kf)):
                    for hd in range(HEADS):
                        last = pe.transpose(bank[b][0:QK, hd * P:(hd + 1) * P], src[:, hd, :], ident)
                last.then_inc(full_turned, 1)
                turn()
                turn_probs(s, fox_s)
                for kt in range(t + 1):
                    for pair in range(HEADS // 2):
                        last = pe.matmul(bank[kt][:, pair * 2 * P:(pair + 1) * 2 * P], kTs[:, pair, kt * P:(kt + 1) * P],
                                         qTs[:, 2 * pair:2 * pair + 2, :], start=True, stop=True)
                last.then_inc(stick_scored, 1)
                turn()
                next_of(probsT_ready, t + 1)
                next_of(full_ready, 2)
                weigh(s, bank[4], probsT, lambda kt, hd: vf[:, kt, hd * HD:(hd + 1) * HD], HD)
                next_of(lom_ready)
                for kt in range(t + 1):
                    last = pe.matmul(bank[2 + kt][:, :], tri_gt, lom[:, kt, :], start=True, stop=(kt == t))
                    for later in range(kt + 1, t + 1):
                        last = pe.matmul(bank[2 + kt][:, :], ones, lom[:, later, :], start=False, stop=(later == t))
                last.then_inc(rest_ready, 1)
                turn()
                head_scores(s, qTm, kTm, QK, False)
                next_of(stick_ready)
                weigh(s, bank[4][:, 256:512], soft, lambda kt, hd: vs[:, kt, hd * HD:(hd + 1) * HD], HD)
                turn()
                turn_probs(s, mla_s)
                turn()
                next_of(probsT_ready, t + 1)
                weigh(s, bank[5], probsT, lambda kt, hd: vm[:, kt, hd, :], VD)
                turn()
                next_of(normed)
                turn_rows(y)
                turn()
                next_of(hT_ready, 2)
                for k in range(KT // 2):
                    w = weights()
                    b0, first, stop = ((2, True, True), (4, True, True), (0, True, False), (0, False, True))[k]
                    for a in range(2):
                        for c in range(2):
                            last = pe.matmul(bank[b0 + c][:, :], hT[:, 2 * k + a, :],
                                             w[:, a * D + c * 512:a * D + c * 512 + 512],
                                             start=(first and a == 0), stop=(stop and a == 1), skip_group_check=True)
                    release(last)
                    turn()
                next_of(normed)
                turn_rows(xc[:, s % 2, :])
                turn()
                next_of(hT_ready, 2)
                for k in range(KT // 2):
                    w = weights()
                    for a in range(2):
                        for hd in range(PH):
                            last = pe.matmul(bank[2 + hd // 4][:, hd % 4 * P:hd % 4 * P + P],
                                             w[:, a * D + hd * P:a * D + (hd + 1) * P], hT[:, 2 * k + a, :],
                                             start=(k == 0 and a == 0 and hd % 4 == 0),
                                             stop=(k == KT // 2 - 1 and a == 1), skip_group_check=True)
                    release(last)
                    turn()
                next_of(query_ready, 2)
                w = weights()
                for hp in range(2 * PH):
                    b = hp % 2 * 64
                    last = pe.matmul(score(hp), queryT[b:b + 64, hp // 2, :], w[b:b + 64, hp // 2 * P:(hp // 2 + 1) * P],
                                     start=True, stop=True)
                release(last)

            def choose(s, c, turn):
                turn()
                turn()

            def lift(s):
                l, t = layer_tile(s)
                if s == 0:
                    pe.wait_ge(late_in, 48)
                w = weights()
                for c in range(2):
                    for k in range(2):
                        last = pe.matmul(bank[4 + c][:, :], pT[:, 2 * l + k, t * P:(t + 1) * P],
                                         w[:, k * D + c * 512:k * D + c * 512 + 512], start=(k == 0), stop=(k == 1))
                release(last)

            def embed(s, turn):
                l, t = layer_tile(s)
                pe.wait_ge(acc_read, 2 * (s + 1))
                turn_rows(h[:, t, :])
                turn()
                next_of(hT_ready, 2)
                for c in range(2):
                    for k in range(KT // 2):
                        w = weights(k if c == 0 else 0)
                        for a in range(2):
                            last = pe.matmul(bank[2 + c][:, :], hT[:, 2 * k + a, :],
                                             w[:, a * D + c * 512:a * D + c * 512 + 512],
                                             start=(k == 0 and a == 0), stop=(k == KT // 2 - 1 and a == 1))
                        if c == 1:
                            release(last)
                        elif k == KT // 2 - 1:
                            last.then_inc(gate_half, 1)
                        if k % 2:
                            turn()

            walk(Stream(pe, experts), {"front": front, "leave": leave, "rest": rest, "choose": choose, "embed": embed, "lift": lift,
                                       "begin": begin, "finish": lambda t: None, "ahead": ahead})

        @block.scalar
        def _(act):
            next_of = waiter(act)

            def experts(step, i, half, unit=GROUP):
                for n, j0 in enumerate(range(half * GROUP, (half + 1) * GROUP, unit)):
                    group = step * GROUPS + 2 * i + half + n + 1
                    act.wait_ge(dotted, step * PAIRS + i * RING + j0 + unit)
                    act.activation(gel[:, j0:j0 + unit], pre[:, j0:j0 + unit], ACT.Gelu).then_inc(gelued, 1)
                    act.wait_ge(gelued, group)
                    for j in range(j0, j0 + unit):
                        last = act.activation(act_w[:, j:j + 1], gate[:, step % 2, bass.ds(i * RING + j, 1)], ACT.Copy,
                                              scale=gel[:, j:j + 1])
                    last.then_inc(weighted, 1)
                    act.wait_ge(weighted, group)
                    for j in range(j0, j0 + unit):
                        act.activation(diag[:, j, :], ident, ACT.Copy, scale=act_w[:, j:j + 1]).then_inc(diag_ready, 1)

            class GatedStream(Stream):
                def __call__(self, step, a, b):
                    if b > a:
                        act.wait_ge(gate_ready, step * CHUNKS + -(-b * GROUP // CHUNK_PAIRS))
                    share_out(self, step, a, b)


            def exps(s, src, slot, scale):
                l, t = layer_tile(s)
                next_of(peak_ready)
                for hd in range(HEADS):
                    act.activation(src[:, hd, 0:(t + 1) * P], src[:, hd, 0:(t + 1) * P], ACT.Exp,
                                   bias=peak[:, slot, hd:hd + 1], scale=scale,
                                   accum_out=den[:, slot, hd:hd + 1]).then_inc(probs_ready, 1)

            def copy_probsT(s):
                l, t = layer_tile(s)
                next_of(probs_turned)
                for kt in range(t + 1):
                    act.activation(probsT[:, kt, :], bank[2 + kt][:, :], ACT.Copy).then_inc(probsT_ready, 1)

            def copy_heads(s):
                l, t = layer_tile(s)
                here = slice(t * P, (t + 1) * P)
                for b, qT, kT in zip(front_banks(s), (qTf, qTs), (kTf, kTs)):
                    q2 = b[:, 0:256].rearrange("p (g c) -> p g c", g=2)
                    pairs = qT[:].rearrange("p (g two) c -> p g two c", two=2)
                    for half in range(2):
                        r = slice(half * HD, (half + 1) * HD)
                        act.activation(pairs[r, :, half, :], q2[r, :, :], ACT.Copy).then_inc(heads_ready, 1)
                    act.activation(kT[:, :, here], b[:, 256:512].rearrange("p (g c) -> p g c", g=2),
                                   ACT.Copy).then_inc(heads_ready, 1)

            ahead_turn = [0]

            def ahead():
                n = ahead_turn[0]
                ahead_turn[0] += 1
                if n == 1:
                    act.wait_ge(angles_ready, 2)
                    act.activation(sin[:], ang[:], ACT.Sin).then_inc(trig_ready, 1)
                    act.activation(cos[:], turns_n[:], ACT.Sin).then_inc(trig_ready, 1)
                if n == 16:
                    next_of(ahead_heads)
                    copy_heads(1)

            def front(s, turn):
                for _ in FRONT:
                    turn()

            def leave(s, turn):
                l, t = layer_tile(s)
                if s == 0:
                    act.wait_ge(zeroed, 3)
                    act.wait_ge(projected, 1)
                elif s == 1:
                    act.wait_ge(slab_used, KT)
                else:
                    wait_products(act, "in", s)
                next_of(forget_in)
                act.activation(zf[:, 2, :], zf[:, 1, :], ACT.Exp, scale=-1.0).then_inc(act_done, 1)
                next_of(act_done)
                act.activation(zf[:, 2, :], zf[:, 2, :], ACT.Ln, bias=1.0).then_inc(forget_ln, 1)
                if s != 1:
                    copy_heads(s)
                next_of(latents_left)
                for dst, b in zip((vf, vs), front_banks(s)[2:]):
                    act.activation(dst[:, t, :], b[:, 0:256], ACT.Copy).then_inc(heads_ready, 1)
                turn()

            def rest(s, turn):
                l, t = layer_tile(s)
                here = slice(t * P, (t + 1) * P)
                turn()
                wait_products(act, "latent", s)
                next_of(latent_r)
                r = inv[:, 1, 1:2]
                for c in range(2):
                    kv = bank[3 + c][:, 0:384].rearrange("p (h c) -> p h c", h=2)
                    act.activation(kf[:, 2 * c:2 * c + 2, 0:NOPE], kv[:, :, 0:NOPE], ACT.Copy, scale=r).then_inc(latent_copied, 1)
                    act.activation(vm[:, t, 2 * c:2 * c + 2, :], kv[:, :, NOPE:NOPE + VD], ACT.Copy,
                                   scale=r).then_inc(latent_copied, 1)
                turn()
                exps(s, fox_s, 0, FOX_SCALE)
                next_of(full_turned)
                act.activation(qTm[0:QK, :, :], bank[4][0:QK, :].rearrange("p (h c) -> p h c", h=HEADS),
                               ACT.Copy).then_inc(full_ready, 1)
                act.activation(kTm[0:QK, :, here], bank[5][0:QK, :].rearrange("p (h c) -> p h c", h=HEADS),
                               ACT.Copy).then_inc(full_ready, 1)
                turn()
                copy_probsT(s)
                next_of(stick_scored)
                for kt in range(t + 1):
                    act.activation(soft[:, kt, :], bank[kt][:, :], ACT.Abs, scale=FOX_SCALE).then_inc(act_done, 1)
                next_of(act_done, t + 1)
                for kt in range(t + 1):
                    act.activation(soft[:, kt, :], soft[:, kt, :], ACT.Exp, scale=-1.0).then_inc(act_done, 1)
                next_of(act_done, t + 1)
                for kt in range(t + 1):
                    act.activation(soft[:, kt, :], soft[:, kt, :], ACT.Ln, bias=1.0).then_inc(soft_ready, 1)
                turn()
                next_of(stick_sum)
                for kt in range(t + 1):
                    act.activation(soft[:, kt, :], logb[:, kt, :], ACT.Exp).then_inc(stick_exp, 1)
                turn()
                exps(s, mla_s, 1, MLA_SCALE)
                turn()
                copy_probsT(s)
                for _ in REST[6:]:
                    turn()
                wait_products(act, "query", s)
                for c in range(2):
                    act.activation(queryT[:, 4 * c:4 * c + 4, :], bank[2 + c][:, :].rearrange("p (h c) -> p h c", h=4),
                                   ACT.Copy).then_inc(query_ready, 1)

            def choose(s, c, turn):
                turn()
                next_of(gate_in)
                part = best_v[:, c * CHUNK_HEADS:(c + 1) * CHUNK_HEADS, :]
                act.activation(part, part, ACT.Exp, scale=ffn_r[:, s % 2:s % 2 + 1]).then_inc(gate_exp, 1)
                turn()

            def embed(s, turn):
                for _ in EMBED:
                    turn()
                act.activation(table_spare[:], ident[:, 0:1], ACT.Sigmoid).then_inc(act_done, 1)
                next_of(act_done)
                next_of(ple_r)
                for c in range(2):
                    if c == 0:
                        next_of(gate_half)
                    else:
                        wait_products(act, "gate", s)
                    act.activation(gate_s[:, c * 512:(c + 1) * 512], bank[2 + c][:, :], ACT.Sigmoid,
                                   scale=inv[:, 1, 0:1]).then_inc(sig_ready, 1)

            walk(GatedStream(act, experts), {"front": front, "leave": leave, "rest": rest, "choose": choose, "embed": embed, "lift": lambda s: None,
                          "begin": lambda w: None, "finish": lambda t: None, "ahead": ahead})

        @block.vector
        def _(dve):
            next_of = waiter(dve)

            def link(ins):
                ins.then_inc(dve_done, 1)
                next_of(dve_done)

            def experts(step, i, half, unit=GROUP):
                for j in range(half * GROUP, half * GROUP + GROUP):
                    dve.wait_ge(row_in[j], (step * (PAIRS // RING) + i + 1) * 16)
                    u = ring[:, j, 0:D]
                    dve.tensor_tensor_reduce(out=u, in0=u, in1=xc[:, step % 2, :], scale=1.0, scalar=0.0,
                                             op0=ALU.mult, op1=ALU.add, accum_out=pre[:, j:j + 1]).then_inc(dotted, 1)

            def rsqrt(sizes, done=dve_done):
                n = len(sizes)
                v, g, a, b = (inv[:, i, 0:n] for i in range(4))
                for i, size in enumerate(sizes):
                    link(dve.tensor_scalar(inv[:, 0, i:i + 1], ssq[:, i:i + 1], 1.0 / size, EPS, ALU.mult, ALU.add))
                link(dve.tensor_scalar(g.bitcast(U32), v.bitcast(U32), 1, None, ALU.logical_shift_right))
                link(dve.tensor_scalar(g.bitcast(I32), g.bitcast(I32), -1.0, float(0x5f3759df), ALU.mult, ALU.add))
                for i in range(3):
                    link(dve.tensor_tensor(a, g, v, ALU.mult))
                    link(dve.scalar_tensor_tensor(out=b, in0=a, scalar=-0.5, in1=g, op0=ALU.mult, op1=ALU.mult))
                    last = dve.scalar_tensor_tensor(out=g, in0=b, scalar=1.5, in1=g, op0=ALU.add, op1=ALU.mult)
                    s = done if i == 2 else dve_done
                    last.then_inc(s, 1)
                    next_of(s)

            def squares(src, i, junk):
                link(dve.tensor_tensor_reduce(out=junk, in0=src, in1=src, scale=1.0, scalar=0.0,
                                              op0=ALU.mult, op1=ALU.add, accum_out=ssq[:, i:i + 1]))

            def norm_rows(src):
                squares(src, 0, rows_n[:, :])
                rsqrt([D])
                dve.tensor_scalar(rows_n[:, :], src, inv[:, 1, 0:1], None, ALU.mult).then_inc(normed, 1)

            def copy_hT(gain, hT=hT):
                next_of(turned)
                for c in range(2):
                    src = bank[c][:, :].rearrange("p (k c) -> p k c", k=4)
                    if gain is None:
                        ins = dve.tensor_copy(hT[:, 4 * c:4 * c + 4, :], src)
                    else:
                        g = gain[:, 4 * c:4 * c + 4].unsqueeze(2).broadcast_to([P, 4, P])
                        ins = dve.tensor_tensor(hT[:, 4 * c:4 * c + 4, :], src, g, ALU.mult)
                    ins.then_inc(hT_ready, 1)

            def peaks(s, dst, slot, scale, fox):
                l, t = layer_tile(s)
                next_of(scored)
                for kt in range(t + 1):
                    src = bank[kt][:, :].rearrange("p (h k) -> p h k", h=HEADS)
                    o = dst[:, :, kt * P:(kt + 1) * P]
                    mask = causal.unsqueeze(1).broadcast_to([P, HEADS, P])
                    if fox:
                        link(dve.tensor_tensor(o, src, F8[:, :].unsqueeze(2).broadcast_to([P, HEADS, P]), ALU.add))
                        if kt == t:
                            link(dve.tensor_tensor(o, o, mask, ALU.add))
                    elif kt == t:
                        link(dve.tensor_tensor(o, src, mask, ALU.add))
                    else:
                        link(dve.tensor_copy(o, src))
                link(dve.tensor_reduce(peak[:, slot, :], dst[:, :, 0:(t + 1) * P], AX_X, ALU.max))
                dve.tensor_scalar(peak[:, slot, :], peak[:, slot, :], -scale, None, ALU.mult).then_inc(peak_ready, 1)

            def normalised(dst, src, slot, width):
                next_of(probs_ready, HEADS)
                link(dve.reciprocal(den[:, slot, :], den[:, slot, :]))
                link(dve.tensor_tensor(dst, src.rearrange("p (h c) -> p h c", h=HEADS),
                                       den[:, slot, :].unsqueeze(2).broadcast_to([P, HEADS, width]), ALU.mult))

            def angles():
                link(dve.tensor_copy(posf[:], posi[:]))
                for t in range(TILES):
                    link(dve.tensor_scalar(ang[:, t, :], cst[:, C_FREQ:C_FREQ + HALF], posf[:, t:t + 1], None, ALU.mult))
                magic = 1.5 * 2.0 ** 23
                link(dve.tensor_scalar(turns_n[:], ang[:], float(1 / (2 * np.pi)), magic, ALU.mult, ALU.add))
                link(dve.tensor_scalar(turns_n[:], turns_n[:], magic, None, ALU.subtract))
                rest = 2 * np.pi
                for bits in (6, 14, 22, None):
                    part = float(np.float32(rest)) if bits is None else float(np.floor(rest * 2.0 ** (bits - 0)) / 2.0 ** (bits - 0))
                    rest -= part
                    link(dve.scalar_tensor_tensor(out=ang[:].rearrange("p t c -> p (t c)"),
                                                  in0=turns_n[:].rearrange("p t c -> p (t c)"), scalar=-part,
                                                  in1=ang[:].rearrange("p t c -> p (t c)"), op0=ALU.mult, op1=ALU.add))
                lim = 3.1415925
                link(dve.tensor_scalar(ang[:], ang[:], lim, -lim, ALU.min, ALU.max))
                a2, n2 = ang[:].rearrange("p t c -> p (t c)"), turns_n[:].rearrange("p t c -> p (t c)")
                dve.scalar_tensor_tensor(out=n2, in0=a2, scalar=-1.0, in1=a2, op0=ALU.mult,
                                         op1=ALU.max).then_inc(angles_ready, 1)
                dve.wait_ge(angles_ready, 1)
                dve.tensor_scalar(n2, n2, -1.0, float(np.pi / 2), ALU.mult, ALU.add).then_inc(angles_ready, 1)

            def front(s, turn):
                l, t = layer_tile(s)
                if s == 0:
                    for a in (qTf, qTs, FT):
                        dve.memset(a[:], 0.0).then_inc(zeroed, 1)
                    dve.wait_ge(zeroed, 3)
                    dve.wait_ge(x_in[0], 16)
                norm_rows(h[:, t, :])
                if s == 0:
                    dve.wait_ge(consts_in, 32)
                turn()
                copy_hT(gn[:, l, G_MIX:G_MIX + KT])
                for _ in FRONT[1:]:
                    turn()

            ahead_turn = [0]

            def ahead():
                n = ahead_turn[0]
                ahead_turn[0] += 1
                if n == 1:
                    dve.wait_ge(small_in, 32)
                    angles()
                    dve.wait_ge(x_in[1], 16)
                    norm_rows(h[:, 1, :])
                if n == 4:
                    copy_hT(gn[:, 0, G_MIX:G_MIX + KT], hT_next)

            def leave(s, turn):
                l, t = layer_tile(s)
                if s == 0:
                    dve.wait_ge(projected, 1)
                elif s == 1:
                    dve.wait_ge(slab_used, KT)
                else:
                    wait_products(dve, "in", s)
                b4, b5 = front_banks(s)[2:]
                z = zf[:, 0, :]
                link(dve.tensor_tensor(z, b4[:, 256:260], fb[:, l, :], ALU.add))
                dve.scalar_tensor_tensor(out=zf[:, 1, :], in0=z, scalar=-1.0, in1=z, op0=ALU.mult,
                                         op1=ALU.max).then_inc(forget_in, 1)
                link(dve.tensor_copy(lat[:, 0:QR], b5[:, 256:512]))
                dve.tensor_copy(lat[:, QR:], b4[:, 260:388]).then_inc(normed, 1)
                dve.tensor_copy(rot[:, HEADS, :], b4[:, 388:420]).then_inc(latents_left, 1)
                next_of(latents_left)
                next_of(forget_ln)
                dve.scalar_tensor_tensor(out=logf[:, t, :], in0=z, scalar=0.0, in1=zf[:, 2, :], op0=ALU.min,
                                         op1=ALU.subtract).then_inc(logf_ready, 1)
                next_of(latent_turned)
                dve.tensor_tensor(latT[:], leave_banks(s)[1][:, 0:384].rearrange("p (k c) -> p k c", k=3),
                                  gn[:, l, G_Q:G_Q + 3].unsqueeze(2).broadcast_to([P, 3, P]),
                                  ALU.mult).then_inc(latT_ready, 1)
                next_of(cum_ready)
                cum = leave_banks(s)[0]
                link(dve.tensor_scalar(F8[:], cum[:, 0:HEADS], 1.0 / FOX_SCALE, None, ALU.mult))
                dve.tensor_copy(FT[0:HEADS, t * P:(t + 1) * P], cum[0:HEADS, P:2 * P]).then_inc(cum_copied, 1)
                squares(lat[:, 0:QR], 0, rows_n[:, 0:QR])
                squares(lat[:, QR:], 1, rows_n[:, QR:QR + KVR])
                rsqrt([QR, KVR], latent_r)
                turn()

            def rest(s, turn):
                l, t = layer_tile(s)
                here = slice(t * P, (t + 1) * P)
                turn()
                wait_products(dve, "latent", s)
                q3 = bank[2][:, 0:384].rearrange("p (h c) -> p h c", h=HEADS)
                r = inv[:, 1, 0:1]
                link(dve.tensor_scalar(rot[:, 0:HEADS, :], q3[:, :, NOPE:QK], r, None, ALU.mult))
                link(dve.tensor_scalar(qf[:, :, 0:NOPE], q3[:, :, 0:NOPE], r, None, ALU.mult))
                if s == 0:
                    dve.wait_ge(trig_ready, 2)
                x1, x2 = rot[:, :, 0:HALF], rot[:, :, HALF:ROPE]
                c_, s_ = (a[:, t, :].unsqueeze(1).broadcast_to([P, HEADS + 1, HALF]) for a in (cos, sin))
                for i, (a, b) in enumerate(((x1, c_), (x2, s_), (x1, s_), (x2, c_))):
                    ins = dve.tensor_tensor(rot_p[:, i], a, b, ALU.mult)
                link(ins)
                dve.tensor_tensor(rotated[:, :, 0:HALF], rot_p[:, 0], rot_p[:, 1], ALU.subtract)
                link(dve.tensor_tensor(rotated[:, :, HALF:ROPE], rot_p[:, 2], rot_p[:, 3], ALU.add))
                dve.tensor_copy(qf[:, :, NOPE:QK], rotated[:, 0:HEADS, :])
                dve.tensor_copy(kf[:, :, NOPE:QK],
                                rotated[:, HEADS:HEADS + 1, :].broadcast_to([P, HEADS, ROPE])).then_inc(rotated_ready, 1)
                turn()
                peaks(s, fox_s, 0, FOX_SCALE, True)
                turn()
                next_of(soft_ready, t + 1)
                for kt in range(t + 1):
                    b = bank[kt][:, :]
                    link(dve.tensor_scalar(logb[:, kt, :], b, FOX_SCALE, 0.0, ALU.mult, ALU.min))
                    link(dve.tensor_tensor(logb[:, kt, :], logb[:, kt, :], soft[:, kt, :], ALU.subtract))
                    link(dve.scalar_tensor_tensor(out=lom[:, kt, :], in0=b, scalar=-FOX_SCALE, in1=logb[:, kt, :],
                                                  op0=ALU.mult, op1=ALU.add))
                strict4 = strict.unsqueeze(1).broadcast_to([P, HEADS, P])
                lom3 = lom[:, t, :].rearrange("p (h q) -> p h q", h=HEADS)
                dve.tensor_tensor(lom3, lom3, strict4, ALU.mult).then_inc(lom_ready, 1)
                turn()
                next_of(attended)
                normalised(y[:, 0:256].rearrange("p (h c) -> p h c", h=HEADS), bank[4][:, 0:256], 0, HD)
                next_of(rest_ready)
                for kt in range(t + 1):
                    ins = dve.tensor_tensor(logb[:, kt, :], logb[:, kt, :], bank[2 + kt][:, :], ALU.add)
                ins.then_inc(stick_sum, 1)
                next_of(stick_exp, t + 1)
                soft3 = soft[:, t, :].rearrange("p (h q) -> p h q", h=HEADS)
                dve.tensor_tensor(soft3, soft3, strict4, ALU.mult).then_inc(stick_ready, 1)
                turn()
                next_of(attended)
                link(dve.tensor_copy(y[:, 256:512], bank[4][:, 256:512]))
                peaks(s, mla_s, 1, MLA_SCALE, False)
                turn()
                turn()
                next_of(attended)
                next_of(probs_ready, HEADS)
                link(dve.reciprocal(den[:, 1, :], den[:, 1, :]))
                dve.tensor_tensor(y[:, 512:1024].rearrange("p (h c) -> p h c", h=HEADS),
                                  bank[5][:, :].rearrange("p (h c) -> p h c", h=HEADS),
                                  den[:, 1, :].unsqueeze(2).broadcast_to([P, HEADS, VD]), ALU.mult).then_inc(normed, 1)
                turn()
                copy_hT(gn[:, l, G_OUT:G_OUT + KT])
                bounds = ((0, 256), (256, 512), (512, 1024))
                for i, (a, b) in enumerate(bounds):
                    squares(y[:, a:b], i, rows_n[:, a:b])
                rsqrt([b - a for a, b in bounds])
                for _ in range(KT // 2):
                    turn()
                for i, (b0, slab) in enumerate(((2, 0), (4, 1), (0, 3))):
                    wait_products(dve, "out", s, slab)
                    for c in range(2):
                        part = h[:, t, c * 512:(c + 1) * 512]
                        link(dve.scalar_tensor_tensor(out=part, in0=bank[b0 + c][:, :], scalar=inv[:, 1, i:i + 1],
                                                      in1=part, op0=ALU.mult, op1=ALU.add))
                if s == 0:
                    dve.wait_ge(late_in, 48)
                xs = xc[:, s % 2, :]
                dve.tensor_tensor(xs, h[:, t, :], gffn[:, l, :], ALU.mult).then_inc(normed, 1)
                turn()
                copy_hT(None)
                squares(h[:, t, :], 0, rows_n[:, :])
                rsqrt([D])
                link(dve.tensor_copy(ffn_r[:, s % 2:s % 2 + 1], inv[:, 1, 0:1]))
                link(dve.tensor_scalar(xs, xs, inv[:, 1, 0:1], None, ALU.mult))
                for _ in range(KT // 2):
                    turn()

            def top16(lists, values, indices, data, spare):
                for i in lists:
                    ins = dve.max(out=values[:, i, 0:8], in_=data(i))
                link(ins)
                for i in lists:
                    dve.max_index(out=indices[:, i, 0:8], in_max=values[:, i, 0:8], in_values=data(i))
                for i in lists:
                    ins = dve.match_replace(out=spare(i), in_to_replace=values[:, i, 0:8], in_values=data(i),
                                            imm_value=-3e38)
                link(ins)
                for i in lists:
                    ins = dve.max(out=values[:, i, 8:16], in_=spare(i))
                link(ins)
                for i in lists:
                    ins = dve.max_index(out=indices[:, i, 8:16], in_max=values[:, i, 8:16], in_values=spare(i))
                link(ins)

            def choose(s, c, turn):
                l, t = layer_tile(s)
                h0, n = c * CHUNK_HEADS, CHUNK_HEADS
                hs = slice(h0, h0 + n)
                if c == 0:
                    wait_products(dve, "keys", s)
                top16(range(2 * h0, 2 * (h0 + n)), top_v, top_i, score, lambda i: wb[:, i * P:(i + 1) * P])
                halves = slice(2 * h0, 2 * (h0 + n))
                link(dve.tensor_copy(top_f[:, halves], top_i[:, halves]))
                pairs = wa[:, h0 * 256:(h0 + n) * 256].rearrange("p (h a b) -> p h a b", h=n, a=TOPK)
                lists = top_v[:, halves].rearrange("p (h two) a -> p h two a", two=2)
                full = [P, n, TOPK, TOPK]
                link(dve.tensor_tensor(pairs, lists[:, :, 0, :].unsqueeze(3).broadcast_to(full),
                                       lists[:, :, 1, :].unsqueeze(2).broadcast_to(full), ALU.add))
                turn()
                top16(range(h0, h0 + n), best_v, best_i, lambda i: wa[:, i * 256:(i + 1) * 256],
                      lambda i: wb[:, i * 256:(i + 1) * 256])
                dve.tensor_scalar(part_i[:, 0, hs], best_i[:, hs], 4, None, ALU.logical_shift_right)
                dve.tensor_scalar(part_i[:, 1, hs], best_i[:, hs], 15, None, ALU.bitwise_and)
                link(dve.tensor_copy(gsum[:, 0, hs], best_v[:, hs, 0]))
                dve.tensor_tensor(best_v[:, hs], best_v[:, hs], gsum[:, 0, hs].unsqueeze(2).broadcast_to([P, n, TOPK]),
                                  ALU.subtract).then_inc(gate_in, 1)
                link(dve.tensor_copy(part_f[:, :, hs], part_i[:, :, hs]))
                names = top_f[:, halves].rearrange("p (h two) a -> p h two a", two=2)
                iota4 = iota.unsqueeze(1).broadcast_to([P, n * TOPK, TOPK]).rearrange("p (h k) a -> p h k a", h=n)
                w4 = [work[:, h0 * 256:(h0 + n) * 256].rearrange("p (h k a) -> p h k a", h=n, k=TOPK)
                      for work in (wa, wb)]
                for half in range(2):
                    ins = dve.tensor_tensor(w4[half], part_f[:, half, hs].unsqueeze(3).broadcast_to(full), iota4,
                                            ALU.is_equal)
                link(ins)
                for half in range(2):
                    ins = dve.tensor_tensor(w4[half], w4[half], names[:, :, half, :].unsqueeze(2).broadcast_to(full),
                                            ALU.mult)
                link(ins)
                for half in range(2):
                    ins = dve.tensor_reduce(part_id[:, half, hs], w4[half], AX_X, ALU.add)
                link(ins)
                a, b = (part_id[:, i, hs].rearrange("p h k -> p (h k)") for i in range(2))
                link(dve.scalar_tensor_tensor(out=a, in0=a, scalar=float(NKEY), in1=b, op0=ALU.mult, op1=ALU.add))
                cols = slice(h0 * TOPK, (h0 + n) * TOPK)
                dve.tensor_scalar(ids[:, s % 2, cols], a, float(l * EXPERTS), None, ALU.add).then_inc(ids_ready, 1)
                next_of(gate_exp)
                link(dve.tensor_reduce(gsum[:, 1, hs], best_v[:, hs], AX_X, ALU.add))
                link(dve.reciprocal(gsum[:, 1, hs], gsum[:, 1, hs]))
                dve.tensor_tensor(gate[:, s % 2, cols].rearrange("p (h k) -> p h k", h=n), best_v[:, hs],
                                  gsum[:, 1, hs].unsqueeze(2).broadcast_to([P, n, TOPK]),
                                  ALU.mult).then_inc(gate_ready, 1)
                turn()

            def begin(w):
                if w == 0:
                    return
                dve.wait_ge(row_used, w * PAIRS)
                for c in range(2):
                    dve.tensor_copy(h[:, (w - 1) % 2, c * 512:(c + 1) * 512], acc[:, c, :]).then_inc(acc_read, 1)
                dve.wait_ge(acc_read, 2 * w)

            def embed(s, turn):
                l, t = layer_tile(s)
                turn()
                copy_hT(gn[:, l, G_PLE:G_PLE + KT])
                squares(h[:, t, :], 0, rows_n[:, :])
                rsqrt([D], ple_r)
                for _ in EMBED[1:]:
                    turn()
                for c in range(2):
                    next_of(sig_ready)
                    g = gate_s[:, c * 512:(c + 1) * 512]
                    part = h[:, t, c * 512:(c + 1) * 512]
                    link(dve.tensor_tensor(g, g, bank[4 + c][:, :], ALU.mult))
                    link(dve.tensor_tensor(part, part, g, ALU.add))

            def finish(t):
                dst = (y, rows_n)[t]
                squares(h[:, t, :], 0, dst[:, :])
                rsqrt([D])
                dve.scalar_tensor_tensor(out=dst[:, :], in0=h[:, t, :], scalar=inv[:, 1, 0:1], in1=gfin[:],
                                         op0=ALU.mult, op1=ALU.mult).then_inc(result_ready, 1)

            walk(Stream(dve, experts), {"front": front, "leave": leave, "rest": rest, "choose": choose, "embed": embed, "lift": lambda s: None,
                                        "begin": begin, "finish": finish, "ahead": ahead})


def constants():
    c = np.zeros((P, C_W), np.float32)
    i = np.arange(P)
    c[:, C_ID:C_ID + P] = np.eye(P)
    c[:, C_LE:C_LE + P] = i[:, None] <= i[None, :]
    c[:, C_GT:C_GT + P] = i[:, None] > i[None, :]
    c[:, C_ONE:C_ONE + P] = 1.0
    c[:, C_CAUSAL:C_CAUSAL + P] = np.where(i[None, :] <= i[:, None], 0.0, NEG)
    c[:, C_STRICT:C_STRICT + P] = i[:, None] < i[None, :]
    for hd in range(HEADS):
        c[hd, C_SEL + hd * P:C_SEL + (hd + 1) * P] = -1.0 / FOX_SCALE
    c[:, C_FREQ:C_FREQ + HALF] = np.float32(10000.0) ** (-np.arange(HALF, dtype=np.float32) / np.float32(HALF))
    c[:, C_IOTA:C_IOTA + TOPK] = np.arange(TOPK)
    return c


def kernel(x, p, positions, norm_mix_g, w_in, b_forget, mla_q_norm_g, w_uq, mla_kv_norm_g, w_ukv,
           mix_out_norm_g, w_o, norm_ffn_g, peer_w_query, peer_sub_keys, peer_u, peer_v,
           w_ple, ple_norm_g, w_ple_gate, final_norm_g):
    import concourse.bacc as bacc
    from concourse.bass_utils import run_bass_kernel_spmd as run

    def slabs(g):
        g = np.asarray(g)
        return g.reshape(DEPTH, -1, P)

    gains = np.concatenate([slabs(norm_mix_g), slabs(mla_q_norm_g), slabs(mla_kv_norm_g),
                            slabs(mix_out_norm_g), slabs(ple_norm_g)], axis=1)
    uq = np.asarray(w_uq).reshape(DEPTH, 2, P, -1).transpose(0, 2, 1, 3).reshape(DEPTH, P, -1)
    arrays = {
        "x": np.asarray(x).reshape(SEQ, D),
        "p_t": np.asarray(p).reshape(DEPTH, SEQ, 256).transpose(0, 2, 1).reshape(DEPTH * 256, SEQ),
        "pos": np.asarray(positions).reshape(TILES, P).T,
        "gains": gains.transpose(2, 0, 1),
        "forget_b": np.asarray(b_forget),
        "ffn_g": np.asarray(norm_ffn_g),
        "final_g": np.asarray(final_norm_g),
        "w_in": np.asarray(w_in),
        "w_latent": np.concatenate([uq, np.asarray(w_ukv)], axis=2),
        "w_out": np.asarray(w_o),
        "w_query": np.asarray(peer_w_query),
        "keys": np.asarray(peer_sub_keys).transpose(0, 2, 4, 1, 3).reshape(DEPTH, P, PH * NKEY),
        "rows": np.concatenate([np.asarray(peer_u), np.asarray(peer_v)], axis=2).reshape(DEPTH * EXPERTS, 2 * D),
        "w_ple": np.asarray(w_ple),
        "w_gate": np.asarray(w_ple_gate),
        "consts": constants(),
    }
    nc = bacc.Bacc("TRN2", target_bir_lowering=False, num_devices=1)
    aps, feed = {}, {}
    for name, a in arrays.items():
        a = np.ascontiguousarray(a)
        feed["in_" + name] = a
        aps[name] = nc.dram_tensor("in_" + name, a.shape, mybir.dt.from_np(a.dtype), kind="ExternalInput").ap()
    out = nc.dram_tensor("out", (SEQ, D), F32, kind="ExternalOutput").ap()
    trunk(nc, out=out, **aps)
    result = run(nc, [feed], core_ids=[0])
    return result.results[0]["out"].reshape(1, SEQ, D)
```

```python
from contextlib import ExitStack

import numpy as np
import concourse.bass as bass
from concourse import mybir

ALU = mybir.AluOpType
ACT = mybir.ActivationFunctionType
AX_X = mybir.AxisListType.X
F32 = mybir.dt.float32
I32 = mybir.dt.int32
U32 = mybir.dt.uint32

P = 128
D = 1024
KT = D // P
SEQ, TILES, DEPTH = 256, 2, 2
STEPS = DEPTH * TILES
HEADS, HD = 4, 64
NOPE, ROPE, VD = 64, 32, 128
QK = NOPE + ROPE
QR, KVR = 256, 128
FOX_SCALE, MLA_SCALE = HD ** -0.5, QK ** -0.5
IN_W = 3 * 256 + 4 + 3 * 256 + QR + KVR + ROPE
EPS = 1e-6
PH, NKEY, TOPK = 8, 128, 16
EXPERTS = NKEY * NKEY
PAIRS = PH * TOPK
RING, GROUP = 8, 4
GROUPS = PAIRS // GROUP
SINGLY = 2
WRING, WSLOT = 4, 2048
NEG = -1e30
HALF = ROPE // 2
C_ID, C_LE, C_GT, C_ONE, C_CAUSAL, C_STRICT, C_SEL, C_FREQ, C_IOTA = 0, 128, 256, 384, 512, 640, 768, 1280, 1296
C_LATER = 1312
C_W = 1440
G_MIX, G_Q, G_KV, G_OUT, G_PLE, G_W = 0, 8, 10, 11, 19, 27

IN_LOADS = [("in", k) for k in range(KT)]
REST_LOADS = [("latent", 0)] + [("out", k) for k in range(KT // 2)] + \
             [("query", k) for k in range(1, KT // 2)] + [("keys", 0)]
EMBED_LOADS = [("ple", 0)] + [("gate", k) for k in range(KT // 2)]
CHUNKS, CHUNK_HEADS = 4, PH // 4
CHUNK_PAIRS = CHUNK_HEADS * TOPK


def layer_tile(s):
    return s // TILES, s % TILES


def weight_order():
    order = [(kind, k, 0) for kind, k in REST_LOADS]
    for w in range(STEPS):
        if w >= 1:
            order += [(kind, k, w - 1) for kind, k in EMBED_LOADS]
        if w + 1 < STEPS:
            order += [(kind, k, w + 1) for kind, k in (IN_LOADS if w >= 1 else []) + REST_LOADS]
    return order + [(kind, k, STEPS - 1) for kind, k in EMBED_LOADS]


FRONT = [1] + [.5] * KT
LEAVE = [1]
REST = [1, 1, 1, 1, 1, 1, 1, 1] + [.5] * (KT // 2) + [1] + [.5] * (KT // 2) + [1]
CHOOSE = [1, 1]
EMBED = [1] + [.5] * 4


def window_turns(w):
    turns = CHOOSE * (CHUNKS - 1) if w == 0 else EMBED
    if w + 1 < STEPS:
        return turns + (FRONT + LEAVE if w >= 1 else []) + REST + CHOOSE * CHUNKS + [1]
    return turns + [.5, .5, 3]


def gate_heads(s, c):
    if s == 0:
        return slice(c * CHUNK_HEADS, (c + 1) * CHUNK_HEADS)
    return slice(0, PH) if c == CHUNKS - 1 else None


class Shares:

    def __init__(self, stream, step):
        self.stream, self.step, self.turns, self.n, self.sent = stream, step, window_turns(step), 0, 0

    def __call__(self):
        self.n += 1
        assert self.n <= len(self.turns)
        a, b = self.sent, round(GROUPS * sum(self.turns[:self.n]) / sum(self.turns))
        self.sent = b
        if self.n == len(self.turns) and self.step == STEPS - 1:
            self.stream(self.step, a, b - SINGLY)
            for g in range(b - SINGLY, b):
                self.stream.last(self.step, g)
        else:
            self.stream(self.step, a, b)


def share_out(stream, step, a, b):
    if a % 2 and a < b:
        stream.group(step, a // 2, 1)
        a += 1
    if b - a >= 4:
        stream.loop(step, a // 2, b // 2)
        a = b // 2 * 2
    while a < b:
        stream.group(step, a // 2, a % 2)
        a += 1


class Stream:

    def __init__(self, eng, body):
        self.eng, self.body = eng, body

    def group(self, step, i, half):
        self.body(step, i, half)

    def loop(self, step, lo, hi):
        with self.eng.Fori(lo, hi) as i:
            for half in range(2):
                self.body(step, i, half)

    def last(self, step, g):
        self.body(step, g // 2, g % 2, 1)

    def __call__(self, step, a, b):
        share_out(self, step, a, b)


def walk(stream, parts):
    def nothing():
        pass

    ahead = parts["ahead"]
    parts["front"](0, ahead)
    parts["leave"](0, ahead)
    parts["rest"](0, ahead)
    parts["choose"](0, 0, ahead)
    parts["leave"](1, nothing)
    for w in range(STEPS):
        parts["begin"](w)
        turn = Shares(stream, w)
        if w == 0:
            for c in range(1, CHUNKS):
                parts["choose"](0, c, turn)
        if w >= 1:
            parts["lift"](w - 1)
            parts["embed"](w - 1, turn)
        if w + 1 < STEPS:
            if w >= 1:
                parts["front"](w + 1, turn)
                parts["leave"](w + 1, turn)
            parts["rest"](w + 1, turn)
            for c in range(CHUNKS):
                parts["choose"](w + 1, c, turn)
        else:
            turn()
            parts["finish"](0)
            turn()
            parts["lift"](w)
        assert turn.n == len(turn.turns) - 1
        turn()
    parts["begin"](STEPS)
    parts["embed"](STEPS - 1, nothing)
    parts["finish"](1)


def trunk(nc, x, p_t, pos, gains, forget_b, ffn_g, final_g, w_in, w_latent, w_out, w_query, keys,
          rows, w_ple, w_gate, consts, out):
    with ExitStack() as ctx:
        def sb(name, shape, dt=F32):
            return ctx.enter_context(nc.sbuf_tensor(name, shape, dt))

        def sem(name):
            return ctx.enter_context(nc.semaphore(name))

        ring = sb("ring", [P, RING, 2 * D])
        wring = sb("wring", [P, WRING, WSLOT])
        h = sb("h", [P, TILES, D])
        rows_n = sb("rows_n", [P, D])
        hT = sb("hT", [P, KT, P])
        y = sb("y", [P, D])
        xc = sb("xc", [P, 2, D])
        wa = sb("wa", [P, 2048])
        wb = sb("wb", [P, 2048])
        cst = sb("cst", [P, C_W])
        gn = sb("gn", [P, DEPTH, G_W])
        fb = sb("fb", [P, DEPTH, HEADS])
        row_gain = sb("row_gain", [P, D])
        held = sb("held", [P, WSLOT])
        pT = sb("pT", [P, DEPTH * 2, SEQ])
        posi = sb("posi", [P, TILES], I32)
        posf = sb("posf", [P, TILES])
        ang = sb("ang", [P, TILES, HALF])
        turns_n = sb("turns_n", [P, TILES, HALF])
        sin = sb("sin", [P, TILES, HALF])
        cos = sb("cos", [P, TILES, HALF])
        qTf = sb("qTf", [P, HEADS, P])
        kTf = sb("kTf", [P, 2, SEQ])
        qTs = sb("qTs", [P, HEADS, P])
        kTs = sb("kTs", [P, 2, SEQ])
        vf = sb("vf", [P, TILES, 256])
        vs = sb("vs", [P, TILES, 256])
        qTm = sb("qTm", [P, HEADS, P])
        kTm = sb("kTm", [P, HEADS, SEQ])
        vm = sb("vm", [P, TILES, HEADS, VD])
        zf = sb("zf", [P, 3, HEADS])
        logf = sb("logf", [P, TILES, HEADS])
        F8 = sb("F8", [P, HEADS])
        FT = sb("FT", [P, SEQ])
        lat = sb("lat", [P, QR + KVR])
        latT = sb("latT", [P, 3, P])
        qf = sb("qf", [P, HEADS, QK])
        kf = sb("kf", [P, HEADS, QK])
        rot = sb("rot", [P, HEADS + 1, ROPE])
        rot_p = sb("rot_p", [P, 4, HEADS + 1, HALF])
        rotated = sb("rotated", [P, HEADS + 1, ROPE])
        peak = sb("peak", [P, 2, HEADS])
        den = sb("den", [P, 2, HEADS])
        ffn_r = sb("ffn_r", [P, 2])
        ssq = sb("ssq", [P, 3])
        inv = sb("inv", [P, 4, 3])
        top_v = sb("top_v", [P, 2 * PH, TOPK])
        top_i = sb("top_i", [P, 2 * PH, TOPK], U32)
        top_f = sb("top_f", [P, 2 * PH, TOPK])
        best_v = sb("best_v", [P, PH, TOPK])
        best_i = sb("best_i", [P, PH, TOPK], U32)
        part_i = sb("part_i", [P, 2, PH, TOPK], U32)
        part_f = sb("part_f", [P, 2, PH, TOPK])
        part_id = sb("part_id", [P, 2, PH, TOPK])
        gsum = sb("gsum", [P, 2, PH])
        gate = sb("gate", [P, 2, PAIRS])
        ids = sb("ids", [P, 2, PAIRS], I32)
        table_spare = sb("table_spare", [P, 1])
        pre = sb("pre", [P, RING])
        gel = sb("gel", [P, RING])
        act_w = sb("act_w", [P, RING])
        diag = sb("diag", [P, RING, P])

        acc = ctx.enter_context(nc.psum_tensor("acc", [P, 2, 512], F32))
        bank = [ctx.enter_context(nc.psum_tensor(f"bank{i}", [P, 512], F32)) for i in range(6)]

        ident = cst[:, C_ID:C_ID + P]
        tri_le = cst[:, C_LE:C_LE + P]
        tri_gt = cst[:, C_GT:C_GT + P]
        ones = cst[:, C_ONE:C_ONE + P]
        causal = cst[:, C_CAUSAL:C_CAUSAL + P]
        strict = cst[:, C_STRICT:C_STRICT + P]
        not_later = cst[:, C_LATER:C_LATER + P]
        iota = cst[:, C_IOTA:C_IOTA + TOPK]
        fox_s = wa[:, 0:1024].rearrange("p (h k) -> p h k", h=HEADS)
        probsT = wa[:, 1024:2048].rearrange("p (t c) -> p t c", t=2)
        soft = wa[:, 0:1024].rearrange("p (t c) -> p t c", t=2)
        logb = wb[:, 0:1024].rearrange("p (t c) -> p t c", t=2)
        lom = wb[:, 1024:2048].rearrange("p (t c) -> p t c", t=2)
        mla_s = wb[:, 0:1024].rearrange("p (h k) -> p h k", h=HEADS)
        gate_s = wb[:, 0:1024]
        hT_next = xc[:, 1, :].rearrange("p (k c) -> p k c", k=KT)
        queryT = y[:, :].rearrange("p (h c) -> p h c", h=PH)

        def score(hp):
            hd, half = divmod(hp, 2)
            return bank[4 * half + hd // 4][:, hd % 4 * P:hd % 4 * P + P]

        x_in = [sem(f"x_in{t}") for t in range(TILES)]
        consts_in = sem("consts_in")
        small_in = sem("small_in")
        late_in = sem("late_in")
        row_gain_in = sem("row_gain_in")
        held_in = sem("held_in")
        weight_in = [sem(f"weight_in{i}") for i in range(WRING)]
        weight_used = sem("weight_used")
        row_in = [sem(f"row_in{i}") for i in range(RING)]
        dotted = sem("dotted")
        gelued = sem("gelued")
        weighted = sem("weighted")
        diag_ready = sem("diag_ready")
        row_used = sem("row_used")
        acc_read = sem("acc_read")
        ids_ready = sem("ids_ready")
        gate_ready = sem("gate_ready")
        dve_done = sem("dve_done")
        act_done = sem("act_done")
        zeroed = sem("zeroed")
        angles_ready = sem("angles_ready")
        trig_ready = sem("trig_ready")
        normed = sem("normed")
        turned = sem("turned")
        hT_ready = sem("hT_ready")
        projected = sem("projected")
        ahead_heads = sem("ahead_heads")
        cum_copied = sem("cum_copied")
        slab_in = [sem(f"slab_in{k}") for k in range(KT)]
        slab_used = sem("slab_used")
        latent_r = sem("latent_r")
        ple_r = sem("ple_r")
        heads_ready = sem("heads_ready")
        forget_in = sem("forget_in")
        forget_ln = sem("forget_ln")
        latents_left = sem("latents_left")
        logf_ready = sem("logf_ready")
        cum_ready = sem("cum_ready")
        latent_turned = sem("latent_turned")
        latT_ready = sem("latT_ready")
        latent_copied = sem("latent_copied")
        rotated_ready = sem("rotated_ready")
        full_turned = sem("full_turned")
        full_ready = sem("full_ready")
        scored = sem("scored")
        peak_ready = sem("peak_ready")
        probs_ready = sem("probs_ready")
        probs_turned = sem("probs_turned")
        probsT_ready = sem("probsT_ready")
        stick_scored = sem("stick_scored")
        soft_ready = sem("soft_ready")
        lom_ready = sem("lom_ready")
        rest_ready = sem("rest_ready")
        stick_sum = sem("stick_sum")
        stick_ready = sem("stick_ready")
        attended = sem("attended")
        group_in = sem("group_in")
        group_turned = sem("group_turned")
        group_hT = sem("group_hT")
        out_half = sem("out_half")
        query_half = sem("query_half")
        keys_half = sem("keys_half")
        query_ready = sem("query_ready")
        gate_in = sem("gate_in")
        gate_exp = sem("gate_exp")
        gate_half = sem("gate_half")
        sig_ready = sem("sig_ready")
        result_ready = sem("result_ready")
        stored = sem("stored")

        def leave_banks(s):
            return (bank[2], bank[3]) if s == 1 else (bank[0], bank[1])

        def out_banks(s):
            b = ((1, 3), (4, 0), (5, 2)) if s == 0 else ((2, 3), (4, 5), (0, 1))
            return [([bank[i] for i in pair], slab) for pair, slab in zip(b, (0, 1, 3))]

        order = weight_order()
        block = ctx.enter_context(nc.Block())

        def wait_products(eng, kind, s, last=KT):
            eng.wait_ge(weight_used, 1 + max(n for n, (a, k, b) in enumerate(order) if (a, b) == (kind, s) and k <= last))

        def front_banks(s):
            return [acc[:, 0, :], acc[:, 1, :], acc[:, 0, :], acc[:, 1, :]] if s == 1 else [b[:, :] for b in bank[2:6]]

        def waiter(eng):
            seen = {}

            def next_of(s, n=1):
                seen[s.name] = seen.get(s.name, 0) + n
                eng.wait_ge(s, seen[s.name])
            return next_of

        @block.sync
        def _(sp):
            def load(dst, src, s):
                sp.dma_start(dst, src).then_inc(s, 16)

            load(h[:, 0, :], x[0:P, :], x_in[0])
            load(cst[:], consts, consts_in)
            load(gn[:], gains, consts_in)
            load(fb[:], forget_b.partition_broadcast(P), small_in)
            load(posi[:], pos, small_in)
            for k in range(KT):
                load(ring[:, k, 0:IN_W], w_in[0, k * P:(k + 1) * P, :], slab_in[k])
                if k == 1:
                    load(h[:, 1, :], x[P:2 * P, :], x_in[1])
            source = {
                "in": lambda l, k: w_in[l, k * P:(k + 1) * P, :],
                "latent": lambda l, k: w_latent[l],
                "out": lambda l, k: w_out[l, 2 * k * P:2 * (k + 1) * P, :].rearrange("(a p) n -> p a n", p=P),
                "query": lambda l, k: w_query[l, 2 * k * P:2 * (k + 1) * P, :].rearrange("(a p) n -> p a n", p=P),
                "gate": lambda l, k: w_gate[l, 2 * k * P:2 * (k + 1) * P, :].rearrange("(a p) n -> p a n", p=P),
                "ple": lambda l, k: w_ple[l].rearrange("(a p) n -> p a n", p=P),
                "keys": lambda l, k: keys[l],
            }
            for n, (kind, k, s) in enumerate(order):
                if n >= WRING:
                    sp.wait_ge(weight_used, n - WRING + 1)
                l, t = layer_tile(s)
                if (kind, k, t) == ("query", 1, 0):
                    if l:
                        sp.wait_ge(ids_ready, CHUNKS * TILES * l)
                    load(held[:].rearrange("p (a n) -> p a n", a=2), source["query"](l, 0), held_in)
                if (kind, k, s) == ("in", 2, TILES):
                    sp.wait_ge(ids_ready, CHUNKS * TILES)
                    load(row_gain[:], ffn_g[1].partition_broadcast(P), row_gain_in)
                if (kind, k, s) == ("gate", 3, STEPS - 2):
                    sp.wait_ge(ids_ready, CHUNKS * STEPS)
                    load(row_gain[:], final_g.partition_broadcast(P), row_gain_in)
                src = source[kind](l, k)
                if len(src.shape) == 3:
                    dst = wring[:, n % WRING, :].rearrange("p (a n) -> p a n", a=2)
                else:
                    dst = wring[:, n % WRING, 0:src.shape[1]]
                sp.dma_start(dst, src).then_inc(weight_in[n % WRING], 16)
                if n == WRING - 1:
                    load(row_gain[:], ffn_g[0].partition_broadcast(P), row_gain_in)
                    load(pT[:], p_t.rearrange("(a p) s -> p a s", p=P), late_in)
            for t in range(TILES):
                for c in range(2):
                    sp.wait_ge(result_ready, 2 * t + c + 1)
                    cols = slice(c * 512, (c + 1) * 512)
                    sp.dma_start(out[t * P:(t + 1) * P, cols], (y, rows_n)[t][:, cols]).then_inc(stored, 16)
            sp.wait_ge(stored, 16 * 2 * TILES)

        @block.gpsimd
        def _(pool):
            for n in range(STEPS * PAIRS):
                w, k = divmod(n, PAIRS)
                if k % CHUNK_PAIRS == 0:
                    pool.wait_ge(ids_ready, n // CHUNK_PAIRS + 1)
                if n < RING:
                    pool.wait_ge(slab_used, n + 1)
                else:
                    pool.wait_ge(row_used, n - RING + 1)
                pool.indirect_dma_start(
                    out=ring[:, n % RING, :], out_offset=None, in_=rows,
                    in_offset=bass.IndirectOffsetOnAxis(ap=ids[:, w % 2, k:k + 1], axis=0),
                ).then_inc(row_in[n % RING], 16)

        @block.tensor
        def _(pe):
            next_of = waiter(pe)
            used = [0]

            def weights(ahead_by=0):
                n = used[0] + ahead_by
                pe.wait_ge(weight_in[n % WRING], 16 * (n // WRING + 1))
                return wring[:, n % WRING, :]

            def release(last):
                used[0] += 1
                last.then_inc(weight_used, 1)

            def experts(step, i, half, unit=GROUP):
                for j in range(half * GROUP, half * GROUP + GROUP):
                    pe.wait_ge(diag_ready, step * PAIRS + i * RING + j + 1)
                    for c in range(2):
                        last = pe.matmul(acc[:, c, :], diag[:, j, :], ring[:, j, D + c * 512:D + c * 512 + 512],
                                         start=False, stop=True, skip_group_check=True)
                    last.then_inc(row_used, 1)

            def begin(w):
                if w == STEPS:
                    return
                if w >= 1:
                    pe.wait_ge(acc_read, 2 * w)
                else:
                    next_of(heads_ready, 2)
                for c in range(2):
                    pe.matmul(acc[:, c, :], ident, h[:, w % 2, c * 512:c * 512 + 512],
                              start=True, stop=True, skip_group_check=True)

            def turn_half(src, half):
                for k in range(half * KT // 2, (half + 1) * KT // 2):
                    last = pe.transpose(bank[half][:, k % 4 * P:k % 4 * P + P], src[:, k * P:(k + 1) * P], ident)
                last.then_inc(turned, 1)

            def turn_rows(src):
                for half in range(2):
                    turn_half(src, half)

            def project(s, part, k, w, hT_s):
                b = front_banks(s)
                a, z = k == 0, k == KT - 1
                if part == 0:
                    for i in range(2):
                        for col in range(4):
                            c0 = 772 * i + col * P
                            last = pe.matmul(b[i][:, col * P:(col + 1) * P], w[:, c0:c0 + P], hT_s[:, k, :],
                                             start=(a and col == 0), stop=z, skip_group_check=True)
                else:
                    pe.matmul(b[2][:, 0:260], hT_s[:, k, :], w[:, 512:772], start=a, stop=z, skip_group_check=True)
                    pe.matmul(b[2][:, 260:420], hT_s[:, k, :], w[:, 1796:1956], start=False, stop=z, skip_group_check=True)
                    last = pe.matmul(b[3][:, :], hT_s[:, k, :], w[:, 1284:1796], start=a, stop=z, skip_group_check=True)
                return last

            def head_scores(s, qT, kT, width, fox):
                l, t = layer_tile(s)
                for kt in range(t + 1):
                    for hd in range(HEADS):
                        o = bank[kt][:, hd * P:(hd + 1) * P]
                        keys_at = slice(kt * P, (kt + 1) * P)
                        if fox:
                            pe.matmul(o, qT[:, hd, :], kT[:, hd // 2, keys_at], start=True, stop=False)
                            last = pe.matmul(o, cst[:, C_SEL + hd * P:C_SEL + (hd + 1) * P], FT[:, keys_at],
                                             start=False, stop=True)
                        else:
                            last = pe.matmul(o, qT[0:width, hd, :], kT[0:width, hd, keys_at], start=True, stop=True)
                last.then_inc(scored, 1)

            def turn_probs(s, src):
                l, t = layer_tile(s)
                next_of(probs_ready, HEADS)
                for kt in range(t + 1):
                    for hd in range(HEADS):
                        last = pe.transpose(bank[2 + kt][:, hd * P:(hd + 1) * P], src[:, hd, kt * P:(kt + 1) * P], ident)
                last.then_inc(probs_turned, 1)

            def weigh(s, dst, src, v, width):
                l, t = layer_tile(s)
                for hd in range(HEADS):
                    for kt in range(t + 1):
                        last = pe.matmul(dst[:, hd * width:(hd + 1) * width], src[:, kt, hd * P:(hd + 1) * P],
                                         v(kt, hd), start=(kt == 0), stop=(kt == t))
                last.then_inc(attended, 1)

            def front(s, turn):
                if s == 0:
                    pe.wait_ge(consts_in, 32)
                next_of(normed)
                turn_rows(rows_n)
                turn()
                for k in range(KT):
                    if k % (KT // 2) == 0:
                        next_of(hT_ready)
                    if s == 0:
                        pe.wait_ge(slab_in[k], 16)
                        w = ring[:, k, :]
                    else:
                        w = weights()
                    project(s, 0, k, w, hT)
                    last = project(s, 1, k, w, hT)
                    if s >= 1:
                        release(last)
                    elif k == KT - 1:
                        last.then_inc(projected, 1)
                    turn()

            ahead_turn = [0]

            def ahead():
                n = ahead_turn[0]
                ahead_turn[0] += 1
                if n == 3:
                    next_of(normed)
                    turn_rows(rows_n)
                first = {9: (0, 2), 10: (2, 3), 11: (3, 5), 12: (5, 8)}.get(n, (0, 0))
                second = {27: (0, 8)}.get(n, (0, 0))
                if n == 9:
                    next_of(hT_ready, 2)
                for k in range(*first):
                    last = project(1, 0, k, ring[:, k, :], hT_next)
                    if k == KT - 1:
                        last.then_inc(ahead_heads, 1)
                if n == 27:
                    next_of(heads_ready, 6)
                for k in range(*second):
                    project(1, 1, k, ring[:, k, :], hT_next).then_inc(slab_used, 1)

            def leave(s, turn):
                l, t = layer_tile(s)
                cum, turned_lat = leave_banks(s)
                next_of(normed)
                for k in range(3):
                    last = pe.transpose(turned_lat[:, k * P:(k + 1) * P], lat[:, k * P:(k + 1) * P], ident)
                last.then_inc(latent_turned, 1)
                if s == 0:
                    turn()
                next_of(logf_ready)
                pe.matmul(cum[:, 0:HEADS], tri_le, logf[:, t, :], start=True, stop=(t == 0))
                if t:
                    pe.matmul(cum[:, 0:HEADS], ones, logf[:, 0, :], start=False, stop=True)
                last = pe.matmul(cum[0:HEADS, P:2 * P], logf[:, t, :], tri_le, start=True, stop=(t == 0))
                if t:
                    last = pe.matmul(cum[0:HEADS, P:2 * P], logf[:, 0, :], ones, start=False, stop=True)
                last.then_inc(cum_ready, 1)
                if s > 0:
                    turn()

            def turn_group(g):
                next_of(group_in)
                for k in (2 * g, 2 * g + 1):
                    last = pe.transpose(bank[5][:, k * P:(k + 1) * P], y[:, k * P:(k + 1) * P], ident)
                last.then_inc(group_turned, 1)

            def project_out(s, k):
                w = weights()
                g = min(k, 2)
                first, stop = k <= 2, k != 2
                for c in range(2):
                    for a in range(2):
                        last = pe.matmul(out_banks(s)[g][0][c][:, :], hT[:, 2 * k + a, :],
                                         w[:, a * D + c * 512:a * D + c * 512 + 512],
                                         start=(first and a == 0), stop=(stop and a == 1), skip_group_check=True)
                    if c == 0 and k == KT // 2 - 1:
                        last.then_inc(out_half, 1)
                release(last)

            def rest(s, turn):
                l, t = layer_tile(s)
                next_of(latT_ready)
                next_of(cum_copied)
                if s != 1:
                    next_of(heads_ready, 8)
                w = weights()
                for k in range(2):
                    pe.matmul(bank[2][:, 0:384], latT[:, k, :], w[:, k * 384:(k + 1) * 384], start=(k == 0), stop=(k == 1))
                for c in range(2):
                    last = pe.matmul(bank[3 + c][:, 0:384], latT[:, 2, :], w[:, 768 + c * 384:768 + (c + 1) * 384],
                                     start=True, stop=True)
                release(last)
                turn()
                head_scores(s, qTf, kTf, HD, True)
                next_of(rotated_ready)
                next_of(latent_copied, 4)
                for b, src in ((4, qf), (5, kf)):
                    for hd in range(HEADS):
                        last = pe.transpose(bank[b][0:QK, hd * P:(hd + 1) * P], src[:, hd, :], ident)
                last.then_inc(full_turned, 1)
                turn()
                turn_probs(s, fox_s)
                for kt in range(t + 1):
                    for pair in range(HEADS // 2):
                        last = pe.matmul(bank[kt][:, pair * 2 * P:(pair + 1) * 2 * P], kTs[:, pair, kt * P:(kt + 1) * P],
                                         qTs[:, 2 * pair:2 * pair + 2, :], start=True, stop=True)
                last.then_inc(stick_scored, 1)
                turn()
                next_of(probsT_ready, t + 1)
                next_of(full_ready, 2)
                weigh(s, bank[4], probsT, lambda kt, hd: vf[:, kt, hd * HD:(hd + 1) * HD], HD)
                next_of(lom_ready)
                for kt in range(t + 1):
                    last = pe.matmul(bank[2 + kt][:, :], tri_gt, lom[:, kt, :], start=True, stop=(kt == t))
                    for later in range(kt + 1, t + 1):
                        last = pe.matmul(bank[2 + kt][:, :], ones, lom[:, later, :], start=False, stop=(later == t))
                last.then_inc(rest_ready, 1)
                turn()
                head_scores(s, qTm, kTm, QK, False)
                if s == 0:
                    turn_group(0)
                next_of(stick_ready, t + 1)
                weigh(s, bank[4][:, 256:512], soft, lambda kt, hd: vs[:, kt, hd * HD:(hd + 1) * HD], HD)
                turn()
                if s == 0:
                    next_of(group_hT)
                    project_out(s, 0)
                    turn_group(1)
                turn_probs(s, mla_s)
                turn()
                next_of(probsT_ready, t + 1)
                if s == 0:
                    next_of(group_hT)
                weigh(s, bank[5], probsT, lambda kt, hd: vm[:, kt, hd, :], VD)
                if s == 0:
                    project_out(s, 1)
                turn()
                next_of(normed)
                if s == 0:
                    for k in range(KT // 2, KT):
                        last = pe.transpose(bank[2][:, k % 4 * P:k % 4 * P + P], y[:, k * P:(k + 1) * P], ident)
                    last.then_inc(turned, 1)
                else:
                    turn_rows(y)
                turn()
                for k in range(KT // 2):
                    if k == KT // 4 or k == 0 and s > 0:
                        next_of(hT_ready)
                    if k >= KT // 4 or s > 0:
                        project_out(s, k)
                    turn()
                for half in range(2):
                    next_of(normed)
                    turn_half(xc[:, s % 2, :], half)
                turn()
                for k in range(KT // 2):
                    if k % (KT // 4) == 0:
                        next_of(hT_ready)
                    if k == 0 and t == 0:
                        next_of(held_in, 16)
                    w = held if k == 0 else weights()
                    for half in range(2):
                        for a in range(2):
                            for hd in range(half * PH // 2, (half + 1) * PH // 2):
                                last = pe.matmul(bank[2 + half][:, hd % 4 * P:hd % 4 * P + P],
                                                 w[:, a * D + hd * P:a * D + (hd + 1) * P], hT[:, 2 * k + a, :],
                                                 start=(k == 0 and a == 0 and hd % 4 == 0),
                                                 stop=(k == KT // 2 - 1 and a == 1), skip_group_check=True)
                        if half == 0 and k == KT // 2 - 1:
                            last.then_inc(query_half, 1)
                    if k:
                        release(last)
                    turn()
                w = weights()
                for hp in range(2 * PH):
                    if hp % PH == 0:
                        next_of(query_ready)
                    b = hp % 2 * 64
                    last = pe.matmul(score(hp), queryT[b:b + 64, hp // 2, :], w[b:b + 64, hp // 2 * P:(hp // 2 + 1) * P],
                                     start=True, stop=True)
                    if hp == PH - 1:
                        last.then_inc(keys_half, 1)
                release(last)
                turn()

            def choose(s, c, turn):
                turn()
                turn()

            def lift(s):
                l, t = layer_tile(s)
                if s == 0:
                    pe.wait_ge(late_in, 16)
                w = weights()
                for c in range(2):
                    for k in range(2):
                        last = pe.matmul(bank[4 + c][:, :], pT[:, 2 * l + k, t * P:(t + 1) * P],
                                         w[:, k * D + c * 512:k * D + c * 512 + 512], start=(k == 0), stop=(k == 1))
                release(last)

            def embed(s, turn):
                l, t = layer_tile(s)
                for half in range(2):
                    pe.wait_ge(acc_read, 2 * s + half + 1)
                    turn_half(h[:, t, :], half)
                turn()
                for c in range(2):
                    for k in range(KT // 2):
                        if c == 0 and k % (KT // 4) == 0:
                            next_of(hT_ready)
                        w = weights(k if c == 0 else 0)
                        for a in range(2):
                            last = pe.matmul(bank[2 + c][:, :], hT[:, 2 * k + a, :],
                                             w[:, a * D + c * 512:a * D + c * 512 + 512],
                                             start=(k == 0 and a == 0), stop=(k == KT // 2 - 1 and a == 1))
                        if c == 1:
                            release(last)
                        elif k == KT // 2 - 1:
                            last.then_inc(gate_half, 1)
                        if k % 2:
                            turn()

            walk(Stream(pe, experts), {"front": front, "leave": leave, "rest": rest, "choose": choose, "embed": embed, "lift": lift,
                                       "begin": begin, "finish": lambda t: None, "ahead": ahead})

        @block.scalar
        def _(act):
            next_of = waiter(act)

            def experts(step, i, half, unit=GROUP):
                for n, j0 in enumerate(range(half * GROUP, (half + 1) * GROUP, unit)):
                    group = step * GROUPS + 2 * i + half + n + 1
                    if unit == 1:
                        group += (GROUP - 1) * (2 * i + half - (GROUPS - SINGLY))
                    act.wait_ge(dotted, step * PAIRS + i * RING + j0 + unit)
                    act.activation(gel[:, j0:j0 + unit], pre[:, j0:j0 + unit], ACT.Gelu).then_inc(gelued, 1)
                    act.wait_ge(gelued, group)
                    for j in range(j0, j0 + unit):
                        last = act.activation(act_w[:, j:j + 1], gate[:, step % 2, bass.ds(i * RING + j, 1)], ACT.Copy,
                                              scale=gel[:, j:j + 1])
                    last.then_inc(weighted, 1)
                    act.wait_ge(weighted, group)
                    for j in range(j0, j0 + unit):
                        act.activation(diag[:, j, :], ident, ACT.Copy, scale=act_w[:, j:j + 1]).then_inc(diag_ready, 1)

            class GatedStream(Stream):
                def __call__(self, step, a, b):
                    if b > a:
                        act.wait_ge(gate_ready, CHUNKS + step if step else -(-b * GROUP // CHUNK_PAIRS))
                    share_out(self, step, a, b)


            def exps(s, src, slot, scale):
                l, t = layer_tile(s)
                next_of(peak_ready)
                for hd in range(HEADS):
                    act.activation(src[:, hd, 0:(t + 1) * P], src[:, hd, 0:(t + 1) * P], ACT.Exp,
                                   bias=peak[:, slot, hd:hd + 1], scale=scale,
                                   accum_out=den[:, slot, hd:hd + 1]).then_inc(probs_ready, 1)

            def copy_probsT(s):
                l, t = layer_tile(s)
                next_of(probs_turned)
                for kt in range(t + 1):
                    act.activation(probsT[:, kt, :], bank[2 + kt][:, :], ACT.Copy).then_inc(probsT_ready, 1)

            def copy_heads(s):
                l, t = layer_tile(s)
                here = slice(t * P, (t + 1) * P)
                for b, qT, kT in zip(front_banks(s), (qTf, qTs), (kTf, kTs)):
                    q2 = b[:, 0:256].rearrange("p (g c) -> p g c", g=2)
                    pairs = qT[:].rearrange("p (g two) c -> p g two c", two=2)
                    for half in range(2):
                        r = slice(half * HD, (half + 1) * HD)
                        act.activation(pairs[r, :, half, :], q2[r, :, :], ACT.Copy).then_inc(heads_ready, 1)
                    act.activation(kT[:, :, here], b[:, 256:512].rearrange("p (g c) -> p g c", g=2),
                                   ACT.Copy).then_inc(heads_ready, 1)

            ahead_turn = [0]

            def ahead():
                n = ahead_turn[0]
                ahead_turn[0] += 1
                if n == 1:
                    act.wait_ge(angles_ready, 2)
                    act.activation(sin[:], ang[:], ACT.Sin).then_inc(trig_ready, 1)
                    act.activation(cos[:], turns_n[:], ACT.Sin).then_inc(trig_ready, 1)
                if n == 16:
                    next_of(ahead_heads)
                    copy_heads(1)

            def front(s, turn):
                for _ in FRONT:
                    turn()

            def leave(s, turn):
                l, t = layer_tile(s)
                if s == 0:
                    act.wait_ge(zeroed, 3)
                    act.wait_ge(projected, 1)
                elif s == 1:
                    act.wait_ge(slab_used, KT)
                else:
                    wait_products(act, "in", s)
                next_of(forget_in)
                act.activation(zf[:, 2, :], zf[:, 1, :], ACT.Exp, scale=-1.0).then_inc(act_done, 1)
                next_of(act_done)
                act.activation(zf[:, 2, :], zf[:, 2, :], ACT.Ln, bias=1.0).then_inc(forget_ln, 1)
                if s != 1:
                    copy_heads(s)
                next_of(latents_left)
                for dst, b in zip((vf, vs), front_banks(s)[2:]):
                    act.activation(dst[:, t, :], b[:, 0:256], ACT.Copy).then_inc(heads_ready, 1)
                turn()

            def rest(s, turn):
                l, t = layer_tile(s)
                here = slice(t * P, (t + 1) * P)
                turn()
                wait_products(act, "latent", s)
                next_of(latent_r)
                r = inv[:, 1, 1:2]
                for c in range(2):
                    kv = bank[3 + c][:, 0:384].rearrange("p (h c) -> p h c", h=2)
                    act.activation(kf[:, 2 * c:2 * c + 2, 0:NOPE], kv[:, :, 0:NOPE], ACT.Copy, scale=r).then_inc(latent_copied, 1)
                    act.activation(vm[:, t, 2 * c:2 * c + 2, :], kv[:, :, NOPE:NOPE + VD], ACT.Copy,
                                   scale=r).then_inc(latent_copied, 1)
                turn()
                exps(s, fox_s, 0, FOX_SCALE)
                next_of(full_turned)
                act.activation(qTm[0:QK, :, :], bank[4][0:QK, :].rearrange("p (h c) -> p h c", h=HEADS),
                               ACT.Copy).then_inc(full_ready, 1)
                act.activation(kTm[0:QK, :, here], bank[5][0:QK, :].rearrange("p (h c) -> p h c", h=HEADS),
                               ACT.Copy).then_inc(full_ready, 1)
                copy_probsT(s)
                next_of(stick_scored)
                for kt in range(t + 1):
                    act.activation(soft[:, kt, :], bank[kt][:, :], ACT.Abs, scale=FOX_SCALE).then_inc(act_done, 1)
                next_of(act_done, t + 1)
                for kt in range(t + 1):
                    act.activation(soft[:, kt, :], soft[:, kt, :], ACT.Exp, scale=-1.0).then_inc(act_done, 1)
                next_of(act_done, t + 1)
                for kt in range(t + 1):
                    act.activation(soft[:, kt, :], soft[:, kt, :], ACT.Ln, bias=1.0).then_inc(soft_ready, 1)
                turn()
                turn()
                next_of(stick_sum)
                for kt in range(t + 1):
                    act.activation(soft[:, kt, :], logb[:, kt, :], ACT.Exp).then_inc(stick_ready, 1)
                turn()
                exps(s, mla_s, 1, MLA_SCALE)
                turn()
                copy_probsT(s)
                for _ in REST[6:-1]:
                    turn()
                for c in range(2):
                    if c == 0:
                        next_of(query_half)
                    else:
                        wait_products(act, "query", s)
                    act.activation(queryT[:, 4 * c:4 * c + 4, :], bank[2 + c][:, :].rearrange("p (h c) -> p h c", h=4),
                                   ACT.Copy).then_inc(query_ready, 1)
                turn()

            def choose(s, c, turn):
                turn()
                next_of(gate_in)
                hs = gate_heads(s, c)
                if hs:
                    act.activation(best_v[:, hs], best_v[:, hs], ACT.Exp,
                                   scale=ffn_r[:, s % 2:s % 2 + 1]).then_inc(gate_exp, 1)
                turn()

            def begin(w):
                if w == 0:
                    act.activation(table_spare[:], ident[:, 0:1], ACT.Gelu).then_inc(act_done, 1)
                    next_of(act_done)

            def embed(s, turn):
                for _ in EMBED:
                    turn()
                act.activation(table_spare[:], ident[:, 0:1], ACT.Sigmoid).then_inc(act_done, 1)
                next_of(act_done)
                next_of(ple_r)
                for c in range(2):
                    if c == 0:
                        next_of(gate_half)
                    else:
                        wait_products(act, "gate", s)
                    act.activation(gate_s[:, c * 512:(c + 1) * 512], bank[2 + c][:, :], ACT.Sigmoid,
                                   scale=inv[:, 1, 0:1]).then_inc(sig_ready, 1)

            walk(GatedStream(act, experts), {"front": front, "leave": leave, "rest": rest, "choose": choose, "embed": embed, "lift": lambda s: None,
                          "begin": begin, "finish": lambda t: None, "ahead": ahead})

        @block.vector
        def _(dve):
            next_of = waiter(dve)

            def link(ins):
                ins.then_inc(dve_done, 1)
                next_of(dve_done)

            def experts(step, i, half, unit=GROUP):
                for j in range(half * GROUP, half * GROUP + GROUP):
                    dve.wait_ge(row_in[j], (step * (PAIRS // RING) + i + 1) * 16)
                    u = ring[:, j, 0:D]
                    dve.tensor_tensor_reduce(out=u, in0=u, in1=xc[:, step % 2, :], scale=1.0, scalar=0.0,
                                             op0=ALU.mult, op1=ALU.add, accum_out=pre[:, j:j + 1]).then_inc(dotted, 1)

            def rsqrt(sizes, done=dve_done):
                n = len(sizes)
                v, g, a, b = (inv[:, i, 0:n] for i in range(4))
                for i, size in enumerate(sizes):
                    link(dve.tensor_scalar(inv[:, 0, i:i + 1], ssq[:, i:i + 1], 1.0 / size, EPS, ALU.mult, ALU.add))
                link(dve.tensor_scalar(g.bitcast(U32), v.bitcast(U32), 1, None, ALU.logical_shift_right))
                link(dve.tensor_scalar(g.bitcast(I32), g.bitcast(I32), -1.0, float(0x5f3759df), ALU.mult, ALU.add))
                for i in range(3):
                    link(dve.tensor_tensor(a, g, v, ALU.mult))
                    link(dve.scalar_tensor_tensor(out=b, in0=a, scalar=-0.5, in1=g, op0=ALU.mult, op1=ALU.mult))
                    last = dve.scalar_tensor_tensor(out=g, in0=b, scalar=1.5, in1=g, op0=ALU.add, op1=ALU.mult)
                    s = done if i == 2 else dve_done
                    last.then_inc(s, 1)
                    next_of(s)

            def squares(src, i, junk):
                link(dve.tensor_tensor_reduce(out=junk, in0=src, in1=src, scale=1.0, scalar=0.0,
                                              op0=ALU.mult, op1=ALU.add, accum_out=ssq[:, i:i + 1]))

            def norm_rows(src):
                squares(src, 0, rows_n[:, :])
                rsqrt([D])
                dve.tensor_scalar(rows_n[:, :], src, inv[:, 1, 0:1], None, ALU.mult).then_inc(normed, 1)

            def copy_hT(gain, hT=hT):
                for c in range(2):
                    next_of(turned)
                    src = bank[c][:, :].rearrange("p (k c) -> p k c", k=4)
                    if gain is None:
                        ins = dve.tensor_copy(hT[:, 4 * c:4 * c + 4, :], src)
                    else:
                        g = gain[:, 4 * c:4 * c + 4].unsqueeze(2).broadcast_to([P, 4, P])
                        ins = dve.tensor_tensor(hT[:, 4 * c:4 * c + 4, :], src, g, ALU.mult)
                    ins.then_inc(hT_ready, 1)

            def peaks(s, dst, slot, scale, fox):
                l, t = layer_tile(s)
                next_of(scored)
                for kt in range(t + 1):
                    src = bank[kt][:, :].rearrange("p (h k) -> p h k", h=HEADS)
                    o = dst[:, :, kt * P:(kt + 1) * P]
                    mask = causal.unsqueeze(1).broadcast_to([P, HEADS, P])
                    if fox:
                        link(dve.tensor_tensor(o, src, F8[:, :].unsqueeze(2).broadcast_to([P, HEADS, P]), ALU.add))
                        if kt == t:
                            link(dve.tensor_tensor(o, o, mask, ALU.add))
                    elif kt == t:
                        link(dve.tensor_tensor(o, src, mask, ALU.add))
                    else:
                        link(dve.tensor_copy(o, src))
                link(dve.tensor_reduce(peak[:, slot, :], dst[:, :, 0:(t + 1) * P], AX_X, ALU.max))
                dve.tensor_scalar(peak[:, slot, :], peak[:, slot, :], -scale, None, ALU.mult).then_inc(peak_ready, 1)

            def copy_group(g, l):
                k = 2 * g
                next_of(group_turned)
                gain = gn[:, l, G_OUT + k:G_OUT + k + 2].unsqueeze(2).broadcast_to([P, 2, P])
                dve.tensor_tensor(hT[:, k:k + 2, :], bank[5][:, k * P:(k + 2) * P].rearrange("p (k c) -> p k c", k=2),
                                  gain, ALU.mult).then_inc(group_hT, 1)

            def normalised(dst, src, slot, width):
                next_of(probs_ready, HEADS)
                link(dve.reciprocal(den[:, slot, :], den[:, slot, :]))
                dve.tensor_tensor(dst, src.rearrange("p (h c) -> p h c", h=HEADS),
                                  den[:, slot, :].unsqueeze(2).broadcast_to([P, HEADS, width]),
                                  ALU.mult).then_inc(group_in, 1)

            def angles():
                link(dve.tensor_copy(posf[:], posi[:]))
                for t in range(TILES):
                    link(dve.tensor_scalar(ang[:, t, :], cst[:, C_FREQ:C_FREQ + HALF], posf[:, t:t + 1], None, ALU.mult))
                magic = 1.5 * 2.0 ** 23
                link(dve.tensor_scalar(turns_n[:], ang[:], float(1 / (2 * np.pi)), magic, ALU.mult, ALU.add))
                link(dve.tensor_scalar(turns_n[:], turns_n[:], magic, None, ALU.subtract))
                rest = 2 * np.pi
                for bits in (6, 14, 22, None):
                    part = float(np.float32(rest)) if bits is None else float(np.floor(rest * 2.0 ** (bits - 0)) / 2.0 ** (bits - 0))
                    rest -= part
                    link(dve.scalar_tensor_tensor(out=ang[:].rearrange("p t c -> p (t c)"),
                                                  in0=turns_n[:].rearrange("p t c -> p (t c)"), scalar=-part,
                                                  in1=ang[:].rearrange("p t c -> p (t c)"), op0=ALU.mult, op1=ALU.add))
                lim = 3.1415925
                link(dve.tensor_scalar(ang[:], ang[:], lim, -lim, ALU.min, ALU.max))
                a2, n2 = ang[:].rearrange("p t c -> p (t c)"), turns_n[:].rearrange("p t c -> p (t c)")
                dve.scalar_tensor_tensor(out=n2, in0=a2, scalar=-1.0, in1=a2, op0=ALU.mult,
                                         op1=ALU.max).then_inc(angles_ready, 1)
                dve.wait_ge(angles_ready, 1)
                dve.tensor_scalar(n2, n2, -1.0, float(np.pi / 2), ALU.mult, ALU.add).then_inc(angles_ready, 1)

            def front(s, turn):
                l, t = layer_tile(s)
                if s == 0:
                    for a in (qTf, qTs, FT):
                        dve.memset(a[:], 0.0).then_inc(zeroed, 1)
                    dve.wait_ge(zeroed, 3)
                    dve.wait_ge(x_in[0], 16)
                norm_rows(h[:, t, :])
                if s == 0:
                    dve.wait_ge(consts_in, 32)
                turn()
                copy_hT(gn[:, l, G_MIX:G_MIX + KT])
                for _ in FRONT[1:]:
                    turn()

            ahead_turn = [0]

            def ahead():
                n = ahead_turn[0]
                ahead_turn[0] += 1
                if n == 1:
                    dve.wait_ge(small_in, 32)
                    angles()
                    dve.wait_ge(x_in[1], 16)
                    norm_rows(h[:, 1, :])
                if n == 4:
                    copy_hT(gn[:, 0, G_MIX:G_MIX + KT], hT_next)

            def leave(s, turn):
                l, t = layer_tile(s)
                if s == 0:
                    dve.wait_ge(projected, 1)
                elif s == 1:
                    dve.wait_ge(slab_used, KT)
                else:
                    wait_products(dve, "in", s)
                b4, b5 = front_banks(s)[2:]
                z = zf[:, 0, :]
                link(dve.tensor_tensor(z, b4[:, 256:260], fb[:, l, :], ALU.add))
                dve.scalar_tensor_tensor(out=zf[:, 1, :], in0=z, scalar=-1.0, in1=z, op0=ALU.mult,
                                         op1=ALU.max).then_inc(forget_in, 1)
                link(dve.tensor_copy(lat[:, 0:QR], b5[:, 256:512]))
                dve.tensor_copy(lat[:, QR:], b4[:, 260:388]).then_inc(normed, 1)
                dve.tensor_copy(rot[:, HEADS, :], b4[:, 388:420]).then_inc(latents_left, 1)
                next_of(latents_left)
                next_of(forget_ln)
                dve.scalar_tensor_tensor(out=logf[:, t, :], in0=z, scalar=0.0, in1=zf[:, 2, :], op0=ALU.min,
                                         op1=ALU.subtract).then_inc(logf_ready, 1)
                next_of(latent_turned)
                dve.tensor_tensor(latT[:], leave_banks(s)[1][:, 0:384].rearrange("p (k c) -> p k c", k=3),
                                  gn[:, l, G_Q:G_Q + 3].unsqueeze(2).broadcast_to([P, 3, P]),
                                  ALU.mult).then_inc(latT_ready, 1)
                next_of(cum_ready)
                cum = leave_banks(s)[0]
                link(dve.tensor_scalar(F8[:], cum[:, 0:HEADS], 1.0 / FOX_SCALE, None, ALU.mult))
                dve.tensor_copy(FT[0:HEADS, t * P:(t + 1) * P], cum[0:HEADS, P:2 * P]).then_inc(cum_copied, 1)
                squares(lat[:, 0:QR], 0, rows_n[:, 0:QR])
                squares(lat[:, QR:], 1, rows_n[:, QR:QR + KVR])
                rsqrt([QR, KVR], latent_r)
                turn()

            def rest(s, turn):
                l, t = layer_tile(s)
                here = slice(t * P, (t + 1) * P)
                turn()
                wait_products(dve, "latent", s)
                q3 = bank[2][:, 0:384].rearrange("p (h c) -> p h c", h=HEADS)
                r = inv[:, 1, 0:1]
                link(dve.tensor_scalar(rot[:, 0:HEADS, :], q3[:, :, NOPE:QK], r, None, ALU.mult))
                link(dve.tensor_scalar(qf[:, :, 0:NOPE], q3[:, :, 0:NOPE], r, None, ALU.mult))
                if s == 0:
                    dve.wait_ge(trig_ready, 2)
                x1, x2 = rot[:, :, 0:HALF], rot[:, :, HALF:ROPE]
                c_, s_ = (a[:, t, :].unsqueeze(1).broadcast_to([P, HEADS + 1, HALF]) for a in (cos, sin))
                for i, (a, b) in enumerate(((x1, c_), (x2, s_), (x1, s_), (x2, c_))):
                    ins = dve.tensor_tensor(rot_p[:, i], a, b, ALU.mult)
                link(ins)
                dve.tensor_tensor(rotated[:, :, 0:HALF], rot_p[:, 0], rot_p[:, 1], ALU.subtract)
                link(dve.tensor_tensor(rotated[:, :, HALF:ROPE], rot_p[:, 2], rot_p[:, 3], ALU.add))
                dve.tensor_copy(qf[:, :, NOPE:QK], rotated[:, 0:HEADS, :])
                dve.tensor_copy(kf[:, :, NOPE:QK],
                                rotated[:, HEADS:HEADS + 1, :].broadcast_to([P, HEADS, ROPE])).then_inc(rotated_ready, 1)
                turn()
                peaks(s, fox_s, 0, FOX_SCALE, True)
                turn()
                next_of(soft_ready, t + 1)
                for kt in range(t + 1):
                    b = bank[kt][:, :]
                    link(dve.tensor_scalar(logb[:, kt, :], b, FOX_SCALE, 0.0, ALU.mult, ALU.min))
                    link(dve.tensor_tensor(logb[:, kt, :], logb[:, kt, :], soft[:, kt, :], ALU.subtract))
                    link(dve.scalar_tensor_tensor(out=lom[:, kt, :], in0=b, scalar=-FOX_SCALE, in1=logb[:, kt, :],
                                                  op0=ALU.mult, op1=ALU.add))
                strict4 = strict.unsqueeze(1).broadcast_to([P, HEADS, P])
                lom3 = lom[:, t, :].rearrange("p (h q) -> p h q", h=HEADS)
                dve.tensor_tensor(lom3, lom3, strict4, ALU.mult).then_inc(lom_ready, 1)
                logb3 = logb[:, t, :].rearrange("p (h q) -> p h q", h=HEADS)
                link(dve.tensor_tensor(logb3, logb3, not_later.unsqueeze(1).broadcast_to([P, HEADS, P]), ALU.add))
                turn()
                next_of(attended)
                normalised(y[:, 0:256].rearrange("p (h c) -> p h c", h=HEADS), bank[4][:, 0:256], 0, HD)
                next_of(rest_ready)
                for kt in range(t + 1):
                    ins = dve.tensor_tensor(logb[:, kt, :], logb[:, kt, :], bank[2 + kt][:, :], ALU.add)
                ins.then_inc(stick_sum, 1)
                if s == 0:
                    copy_group(0, l)
                turn()
                next_of(attended)
                dve.tensor_copy(y[:, 256:512], bank[4][:, 256:512]).then_inc(group_in, 1)
                peaks(s, mla_s, 1, MLA_SCALE, False)
                if s == 0:
                    copy_group(1, l)
                turn()
                turn()
                next_of(attended)
                next_of(probs_ready, HEADS)
                link(dve.reciprocal(den[:, 1, :], den[:, 1, :]))
                dve.tensor_tensor(y[:, 512:1024].rearrange("p (h c) -> p h c", h=HEADS),
                                  bank[5][:, :].rearrange("p (h c) -> p h c", h=HEADS),
                                  den[:, 1, :].unsqueeze(2).broadcast_to([P, HEADS, VD]), ALU.mult).then_inc(normed, 1)
                turn()
                if s == 0:
                    next_of(turned)
                    dve.tensor_tensor(hT[:, KT // 2:, :], bank[2][:, :].rearrange("p (k c) -> p k c", k=4),
                                      gn[:, l, G_OUT + KT // 2:G_OUT + KT].unsqueeze(2).broadcast_to([P, 4, P]),
                                      ALU.mult).then_inc(hT_ready, 1)
                else:
                    copy_hT(gn[:, l, G_OUT:G_OUT + KT])
                next_of(group_in, 2)
                bounds = ((0, 256), (256, 512), (512, 1024))
                for i, (a, b) in enumerate(bounds):
                    squares(y[:, a:b], i, rows_n[:, a:b])
                rsqrt([b - a for a, b in bounds])
                for _ in range(KT // 2):
                    turn()
                if t == 0:
                    next_of(row_gain_in, 16)
                xs = xc[:, s % 2, :]
                for i, (banks, slab) in enumerate(out_banks(s)):
                    if i < 2:
                        wait_products(dve, "out", s, slab)
                    for c in range(2):
                        if i == 2 and c == 0:
                            next_of(out_half)
                        elif i == 2:
                            wait_products(dve, "out", s, slab)
                        part = h[:, t, c * 512:(c + 1) * 512]
                        link(dve.scalar_tensor_tensor(out=part, in0=banks[c][:, :], scalar=inv[:, 1, i:i + 1],
                                                      in1=part, op0=ALU.mult, op1=ALU.add))
                        if i == 2:
                            dve.tensor_tensor(xs[:, c * 512:(c + 1) * 512], part, row_gain[:, c * 512:(c + 1) * 512],
                                              ALU.mult).then_inc(normed, 1)
                turn()
                copy_hT(None)
                squares(h[:, t, :], 0, rows_n[:, :])
                rsqrt([D])
                link(dve.tensor_copy(ffn_r[:, s % 2:s % 2 + 1], inv[:, 1, 0:1]))
                link(dve.tensor_scalar(xs, xs, inv[:, 1, 0:1], None, ALU.mult))
                for _ in range(KT // 2 + 1):
                    turn()

            def top16(lists, values, indices, data, spare):
                for i in lists:
                    ins = dve.max(out=values[:, i, 0:8], in_=data(i))
                link(ins)
                for i in lists:
                    dve.max_index(out=indices[:, i, 0:8], in_max=values[:, i, 0:8], in_values=data(i))
                for i in lists:
                    ins = dve.match_replace(out=spare(i), in_to_replace=values[:, i, 0:8], in_values=data(i),
                                            imm_value=-3e38)
                link(ins)
                for i in lists:
                    ins = dve.max(out=values[:, i, 8:16], in_=spare(i))
                link(ins)
                for i in lists:
                    ins = dve.max_index(out=indices[:, i, 8:16], in_max=values[:, i, 8:16], in_values=spare(i))
                link(ins)

            def choose(s, c, turn):
                l, t = layer_tile(s)
                h0, n = c * CHUNK_HEADS, CHUNK_HEADS
                hs = slice(h0, h0 + n)
                if c == 0:
                    next_of(keys_half)
                elif c == CHUNKS // 2:
                    wait_products(dve, "keys", s)
                top16(range(2 * h0, 2 * (h0 + n)), top_v, top_i, score, lambda i: wb[:, i * P:(i + 1) * P])
                halves = slice(2 * h0, 2 * (h0 + n))
                link(dve.tensor_copy(top_f[:, halves], top_i[:, halves]))
                pairs = wa[:, h0 * 256:(h0 + n) * 256].rearrange("p (h a b) -> p h a b", h=n, a=TOPK)
                lists = top_v[:, halves].rearrange("p (h two) a -> p h two a", two=2)
                full = [P, n, TOPK, TOPK]
                link(dve.tensor_tensor(pairs, lists[:, :, 0, :].unsqueeze(3).broadcast_to(full),
                                       lists[:, :, 1, :].unsqueeze(2).broadcast_to(full), ALU.add))
                if s == 0:
                    turn()
                top16(range(h0, h0 + n), best_v, best_i, lambda i: wa[:, i * 256:(i + 1) * 256],
                      lambda i: wb[:, i * 256:(i + 1) * 256])
                if s > 0:
                    turn()
                dve.tensor_scalar(part_i[:, 0, hs], best_i[:, hs], 4, None, ALU.logical_shift_right)
                dve.tensor_scalar(part_i[:, 1, hs], best_i[:, hs], 15, None, ALU.bitwise_and)
                link(dve.tensor_copy(gsum[:, 0, hs], best_v[:, hs, 0]))
                dve.tensor_tensor(best_v[:, hs], best_v[:, hs], gsum[:, 0, hs].unsqueeze(2).broadcast_to([P, n, TOPK]),
                                  ALU.subtract).then_inc(gate_in, 1)
                link(dve.tensor_copy(part_f[:, :, hs], part_i[:, :, hs]))
                names = top_f[:, halves].rearrange("p (h two) a -> p h two a", two=2)
                iota4 = iota.unsqueeze(1).broadcast_to([P, n * TOPK, TOPK]).rearrange("p (h k) a -> p h k a", h=n)
                w4 = [work[:, h0 * 256:(h0 + n) * 256].rearrange("p (h k a) -> p h k a", h=n, k=TOPK)
                      for work in (wa, wb)]
                for half in range(2):
                    ins = dve.tensor_tensor(w4[half], part_f[:, half, hs].unsqueeze(3).broadcast_to(full), iota4,
                                            ALU.is_equal)
                link(ins)
                for half in range(2):
                    ins = dve.tensor_tensor(w4[half], w4[half], names[:, :, half, :].unsqueeze(2).broadcast_to(full),
                                            ALU.mult)
                link(ins)
                for half in range(2):
                    ins = dve.tensor_reduce(part_id[:, half, hs], w4[half], AX_X, ALU.add)
                link(ins)
                a, b = (part_id[:, i, hs].rearrange("p h k -> p (h k)") for i in range(2))
                link(dve.scalar_tensor_tensor(out=a, in0=a, scalar=float(NKEY), in1=b, op0=ALU.mult, op1=ALU.add))
                cols = slice(h0 * TOPK, (h0 + n) * TOPK)
                dve.tensor_scalar(ids[:, s % 2, cols], a, float(l * EXPERTS), None, ALU.add).then_inc(ids_ready, 1)
                hs = gate_heads(s, c)
                if hs:
                    n = hs.stop - hs.start
                    next_of(gate_exp)
                    link(dve.tensor_reduce(gsum[:, 1, hs], best_v[:, hs], AX_X, ALU.add))
                    link(dve.reciprocal(gsum[:, 1, hs], gsum[:, 1, hs]))
                    dve.tensor_tensor(gate[:, s % 2].rearrange("p (h k) -> p h k", k=TOPK)[:, hs], best_v[:, hs],
                                      gsum[:, 1, hs].unsqueeze(2).broadcast_to([P, n, TOPK]),
                                      ALU.mult).then_inc(gate_ready, 1)
                turn()

            def begin(w):
                if w == 0:
                    return
                dve.wait_ge(row_used, w * PAIRS)
                for c in range(2):
                    dve.tensor_copy(h[:, (w - 1) % 2, c * 512:(c + 1) * 512], acc[:, c, :]).then_inc(acc_read, 1)
                dve.wait_ge(acc_read, 2 * w)

            def embed(s, turn):
                l, t = layer_tile(s)
                turn()
                copy_hT(gn[:, l, G_PLE:G_PLE + KT])
                squares(h[:, t, :], 0, rows_n[:, :])
                rsqrt([D], ple_r)
                for _ in EMBED[1:]:
                    turn()
                for c in range(2):
                    next_of(sig_ready)
                    g = gate_s[:, c * 512:(c + 1) * 512]
                    part = h[:, t, c * 512:(c + 1) * 512]
                    link(dve.tensor_tensor(g, g, bank[4 + c][:, :], ALU.mult))
                    link(dve.tensor_tensor(part, part, g, ALU.add))
                    if l == DEPTH - 1:
                        squares(part, 1 + c, rows_n[:, c * 512:(c + 1) * 512])

            def finish(t):
                link(dve.tensor_tensor(ssq[:, 0:1], ssq[:, 1:2], ssq[:, 2:3], ALU.add))
                rsqrt([D])
                if t == 0:
                    next_of(row_gain_in, 16)
                for c in range(2):
                    cols = slice(c * 512, (c + 1) * 512)
                    dve.scalar_tensor_tensor(out=(y, rows_n)[t][:, cols], in0=h[:, t, cols], scalar=inv[:, 1, 0:1],
                                             in1=row_gain[:, cols], op0=ALU.mult, op1=ALU.mult).then_inc(result_ready, 1)

            walk(Stream(dve, experts), {"front": front, "leave": leave, "rest": rest, "choose": choose, "embed": embed, "lift": lambda s: None,
                                        "begin": begin, "finish": finish, "ahead": ahead})


def constants():
    c = np.zeros((P, C_W), np.float32)
    i = np.arange(P)
    c[:, C_ID:C_ID + P] = np.eye(P)
    c[:, C_LE:C_LE + P] = i[:, None] <= i[None, :]
    c[:, C_GT:C_GT + P] = i[:, None] > i[None, :]
    c[:, C_ONE:C_ONE + P] = 1.0
    c[:, C_CAUSAL:C_CAUSAL + P] = np.where(i[None, :] <= i[:, None], 0.0, NEG)
    c[:, C_STRICT:C_STRICT + P] = i[:, None] < i[None, :]
    c[:, C_LATER:C_LATER + P] = np.where(i[:, None] < i[None, :], 0.0, NEG)
    for hd in range(HEADS):
        c[hd, C_SEL + hd * P:C_SEL + (hd + 1) * P] = -1.0 / FOX_SCALE
    c[:, C_FREQ:C_FREQ + HALF] = np.float32(10000.0) ** (-np.arange(HALF, dtype=np.float32) / np.float32(HALF))
    c[:, C_IOTA:C_IOTA + TOPK] = np.arange(TOPK)
    return c


def kernel(x, p, positions, norm_mix_g, w_in, b_forget, mla_q_norm_g, w_uq, mla_kv_norm_g, w_ukv,
           mix_out_norm_g, w_o, norm_ffn_g, peer_w_query, peer_sub_keys, peer_u, peer_v,
           w_ple, ple_norm_g, w_ple_gate, final_norm_g):
    import concourse.bacc as bacc
    from concourse.bass_utils import run_bass_kernel_spmd as run

    def slabs(g):
        g = np.asarray(g)
        return g.reshape(DEPTH, -1, P)

    gains = np.concatenate([slabs(norm_mix_g), slabs(mla_q_norm_g), slabs(mla_kv_norm_g),
                            slabs(mix_out_norm_g), slabs(ple_norm_g)], axis=1)
    uq = np.asarray(w_uq).reshape(DEPTH, 2, P, -1).transpose(0, 2, 1, 3).reshape(DEPTH, P, -1)
    arrays = {
        "x": np.asarray(x).reshape(SEQ, D),
        "p_t": np.asarray(p).reshape(DEPTH, SEQ, 256).transpose(0, 2, 1).reshape(DEPTH * 256, SEQ),
        "pos": np.asarray(positions).reshape(TILES, P).T,
        "gains": gains.transpose(2, 0, 1),
        "forget_b": np.asarray(b_forget),
        "ffn_g": np.asarray(norm_ffn_g),
        "final_g": np.asarray(final_norm_g),
        "w_in": np.asarray(w_in),
        "w_latent": np.concatenate([uq, np.asarray(w_ukv)], axis=2),
        "w_out": np.asarray(w_o),
        "w_query": np.asarray(peer_w_query),
        "keys": np.asarray(peer_sub_keys).transpose(0, 2, 4, 1, 3).reshape(DEPTH, P, PH * NKEY),
        "rows": np.concatenate([np.asarray(peer_u), np.asarray(peer_v)], axis=2).reshape(DEPTH * EXPERTS, 2 * D),
        "w_ple": np.asarray(w_ple),
        "w_gate": np.asarray(w_ple_gate),
        "consts": constants(),
    }
    nc = bacc.Bacc("TRN2", target_bir_lowering=False, num_devices=1)
    aps, feed = {}, {}
    for name, a in arrays.items():
        a = np.ascontiguousarray(a)
        feed["in_" + name] = a
        aps[name] = nc.dram_tensor("in_" + name, a.shape, mybir.dt.from_np(a.dtype), kind="ExternalInput").ap()
    out = nc.dram_tensor("out", (SEQ, D), F32, kind="ExternalOutput").ap()
    trunk(nc, out=out, **aps)
    result = run(nc, [feed], core_ids=[0])
    return result.results[0]["out"].reshape(1, SEQ, D)
```
